# Optimizing a Trainium2 kernel written in Bass

```python
import jax, jax.numpy as jnp
from jax import lax
import numpy as np

D_MODEL = 1024
BATCH = 1
SEQ = 1024
DEPTH = 1

CHUNK = 64
Q_BLOCK = 2 * CHUNK
D_MIX = D_MODEL
D_CONV = D_MIX // 4
D_POOL = D_MIX // 4
D_ATTN = D_MIX // 2
N_HEADS = 8
HEAD_DIM = D_ATTN // N_HEADS
CONV_K = 31
POOL_WINDOWS = (2, 4, 8, 16)
N_POOL_GROUPS = len(POOL_WINDOWS)
POOL_GROUP = D_POOL // N_POOL_GROUPS
D_FF = ((8 * D_MODEL // 3 + 127) // 128) * 128
FFN_CONV_K = 3
D_IN = 2 * D_CONV + D_POOL + 3 * D_ATTN
EPS = 1e-6

kernel_name = "hybrid_conv_pool_stickbreak_block"

def rmsnorm(x, g):
    xf = x.astype(jnp.float32)
    y = xf * lax.rsqrt(jnp.mean(xf * xf, axis=-1, keepdims=True) + EPS)
    return (y * g.astype(jnp.float32)).astype(x.dtype)

def layernorm(x, g, b):
    xf = x.astype(jnp.float32)
    mu = jnp.mean(xf, axis=-1, keepdims=True)
    var = jnp.mean(jnp.square(xf - mu), axis=-1, keepdims=True)
    y = (xf - mu) * lax.rsqrt(var + EPS)
    return (y * g.astype(jnp.float32) + b.astype(jnp.float32)).astype(x.dtype)

def causal_dwconv(x, w, b):
    k, c = w.shape
    y = lax.conv_general_dilated(
        x, w[:, None, :].astype(x.dtype), window_strides=(1,), padding=[(k - 1, 0)],
        dimension_numbers=("NWC", "WIO", "NWC"), feature_group_count=c)
    return y + b.astype(x.dtype)

def conformer_conv(a, gate, dw_w, dw_b, ln_g, ln_b, pw_w, pw_b):
    u = a * jax.nn.sigmoid(gate)
    u = causal_dwconv(u, dw_w, dw_b)
    u = jax.nn.silu(layernorm(u, ln_g, ln_b))
    return u @ pw_w + pw_b

def multiscale_pool(u, w, scale):
    b, s, _ = u.shape
    uf = u.astype(jnp.float32)
    cs = jnp.cumsum(uf, axis=1)
    count = jnp.arange(1, s + 1, dtype=jnp.float32)[None, :, None]
    groups = []
    for g, win in enumerate(POOL_WINDOWS):
        sl = slice(g * POOL_GROUP, (g + 1) * POOL_GROUP)
        c = cs[..., sl]
        lag = jnp.pad(c, ((0, 0), (win, 0), (0, 0)))[:, :s]
        groups.append((c - lag) / jnp.minimum(count, float(win)) - uf[..., sl])
    p = jnp.stack(groups, axis=2).astype(u.dtype)
    y = jnp.einsum("bsgc,gcd->bsgd", p, w).reshape(b, s, D_POOL)
    return y * scale

def stick_breaking_attention(q, k, v):
    s_len = q.shape[2]
    scale = HEAD_DIM ** -0.5
    outs = []
    for i0 in range(0, s_len, Q_BLOCK):
        kv = i0 + Q_BLOCK
        z = jnp.einsum("bhqd,bhkd->bhqk", q[:, :, i0:kv], k[:, :, :kv]).astype(jnp.float32) * scale
        t_pos = i0 + jnp.arange(Q_BLOCK)[:, None]
        s_pos = jnp.arange(kv)[None, :]
        mask = s_pos < t_pos
        log_keep = jnp.where(mask, jax.nn.log_sigmoid(-z), 0.0)
        log_stick = lax.cumsum(log_keep, axis=3, reverse=True) - log_keep
        a = jnp.where(mask, jnp.exp(jax.nn.log_sigmoid(z) + log_stick), 0.0)
        outs.append(jnp.einsum("bhqk,bhkd->bhqd", a.astype(v.dtype), v[:, :, :kv]))
    return jnp.concatenate(outs, axis=2)

def setup_inputs(seed: int = 0) -> dict:
    key = jax.random.key(seed)
    ks = jax.random.split(key, 20)
    f32 = jnp.float32
    nrm = lambda k, shape, s: jax.random.normal(k, shape, f32) * s
    return {
        "x": jax.random.normal(ks[0], (BATCH, SEQ, D_MODEL), f32),
        "norm1_g": 1.0 + nrm(ks[1], (DEPTH, D_MODEL), 0.05),
        "w_in": nrm(ks[2], (DEPTH, D_MODEL, D_IN), D_MODEL ** -0.5),
        "conv_dw_w": nrm(ks[3], (DEPTH, CONV_K, D_CONV), CONV_K ** -0.5),
        "conv_dw_b": nrm(ks[4], (DEPTH, D_CONV), 0.02),
        "conv_ln_g": 1.0 + nrm(ks[5], (DEPTH, D_CONV), 0.05),
        "conv_ln_b": nrm(ks[6], (DEPTH, D_CONV), 0.02),
        "conv_pw_w": nrm(ks[7], (DEPTH, D_CONV, D_CONV), D_CONV ** -0.5),
        "conv_pw_b": nrm(ks[8], (DEPTH, D_CONV), 0.02),
        "pool_w": nrm(ks[9], (DEPTH, N_POOL_GROUPS, POOL_GROUP, POOL_GROUP), POOL_GROUP ** -0.5),
        "pool_scale": 1.0 + nrm(ks[10], (DEPTH, D_POOL), 0.1),
        "w_out": nrm(ks[11], (DEPTH, D_MIX, D_MODEL), D_MIX ** -0.5),
        "norm2_g": 1.0 + nrm(ks[12], (DEPTH, D_MODEL), 0.05),
        "ffn_up": nrm(ks[13], (DEPTH, D_MODEL, 2 * D_FF), D_MODEL ** -0.5),
        "ffn_dw_w": nrm(ks[14], (DEPTH, FFN_CONV_K, D_FF), FFN_CONV_K ** -0.5),
        "ffn_dw_b": nrm(ks[15], (DEPTH, D_FF), 0.02),
        "ffn_down": nrm(ks[16], (DEPTH, D_FF, D_MODEL), D_FF ** -0.5),
        "final_g": 1.0 + nrm(ks[17], (D_MODEL,), 0.05),
    }

def reference(x, norm1_g, w_in, conv_dw_w, conv_dw_b, conv_ln_g, conv_ln_b, conv_pw_w,
              conv_pw_b, pool_w, pool_scale, w_out, norm2_g, ffn_up, ffn_dw_w, ffn_dw_b,
              ffn_down, final_g):
    b, s, _ = x.shape
    split_at = np.cumsum([D_CONV, D_CONV, D_POOL, D_ATTN, D_ATTN]).tolist()
    for l in range(DEPTH):
        h = rmsnorm(x, norm1_g[l])
        proj = h @ w_in[l]
        c_a, c_g, p_in, q, k, v = jnp.split(proj, split_at, axis=-1)
        y_conv = conformer_conv(c_a, c_g, conv_dw_w[l], conv_dw_b[l], conv_ln_g[l],
                                conv_ln_b[l], conv_pw_w[l], conv_pw_b[l])
        y_pool = multiscale_pool(p_in, pool_w[l], pool_scale[l])
        heads = lambda t: t.reshape(b, s, N_HEADS, HEAD_DIM).transpose(0, 2, 1, 3)
        y_attn = stick_breaking_attention(heads(q), heads(k), heads(v))
        y_attn = y_attn.transpose(0, 2, 1, 3).reshape(b, s, D_ATTN)
        mix = jnp.concatenate([y_conv, y_pool, y_attn], axis=-1)
        x = x + mix @ w_out[l]
        h2 = rmsnorm(x, norm2_g[l])
        val, gate = jnp.split(h2 @ ffn_up[l], 2, axis=-1)
        gate = jax.nn.gelu(causal_dwconv(gate, ffn_dw_w[l], ffn_dw_b[l]), approximate=False)
        x = x + (val * gate) @ ffn_down[l]
    return rmsnorm(x, final_g)


_drawn_inputs = setup_inputs


def setup_inputs(seed=0):
    import zlib

    import numpy as np

    out = dict(_drawn_inputs(seed))
    spreads = {}
    factors = {'conv_dw_b': 5.548,
     'conv_ln_g': 3.306,
     'conv_ln_b': 8.0,
     'conv_pw_b': 6.597,
     'ffn_dw_b': 5.833}
    for name, (base, spread) in spreads.items():
        noise = np.random.default_rng([zlib.crc32(name.encode()), seed]).standard_normal(out[name].shape)
        drawn = base * np.exp(spread * noise) if base else spread * noise
        out[name] = __import__('jax').numpy.asarray(drawn.astype(out[name].dtype))
    for name, factor in factors.items():
        out[name] = (out[name] * factor).astype(out[name].dtype)
    return out
```

```python
from contextlib import ExitStack

import concourse.bass as bass
from concourse import mybir

F32 = mybir.dt.float32
F32R = mybir.dt.float32r
ALU = mybir.AluOpType
ACT = mybir.ActivationFunctionType

P = 128
S = 1024
D = 1024
KT = D // P
TT = S // P
CH = 512
UC = 256
UW = KT * UC
HEADS = 8
PAIRS = HEADS // 2
DH = 64
CONV_K = 31
POOL_WINDOWS = (2, 4, 8, 16)
PAD = max(POOL_WINDOWS)
D_CONV = 256
D_FF = 2816
FT = D_FF // P
NG = FT // 2
EPS = 1e-6
MASK = -float(2 ** 17)
SCALE = DH ** -0.5

VEC = {}
_at = 0
for _name, _n in (("g1", KT), ("g2", KT), ("conv_w", 2 * CONV_K), ("conv_b", 2), ("ln_g", 2), ("ln_b", 2),
                  ("pw_b", 2), ("pool_scale", 2), ("inv_win", 2), ("count_fix", 2 * PAD),
                  ("ffn_w", 3 * FT), ("ffn_b", FT)):
    VEC[_name] = _at
    _at += _n
NVEC = _at

U_GATE, U_A, U_POOL, U_V0, U_V1, U_QK = 0, 1, 2, 3, 4, 5
U_OUT = U_QK + PAIRS
U_FFN_GATE0, U_FFN_VAL0 = U_OUT + 4, U_OUT + 5
U_FFN = U_FFN_VAL0 + 1
NUNITS = U_FFN + 3 * (NG - 1) + 1
J_MIX = U_OUT + 2
NMIXJ = 4
J_OUT2 = J_MIX + NMIXJ
J_FFN_GATE0 = J_OUT2 + 2
J_FFN_VAL0 = J_FFN_GATE0 + 1
J_FFN = J_FFN_VAL0 + 1
J_DOWN_LAST = J_FFN + 3 * (NG - 1)

PJ_QK0 = 3 * 4 + 2 * TT
PJ_POOL_MM = 12 + TT + 3
PJ_LOOP = PJ_QK0 + 4
PJ_OUT = PJ_LOOP + 4 * (PAIRS - 1)


def score_units(i):
    n = max(P * (i + 1), 256)
    if n <= CH:
        return [(0, n)]
    first = CH if n - CH >= 256 else n - 256
    return [(0, first), (first, n - first)]


def unit_index(a, i, u):
    return 12 * a + (i if i < 4 else 4 + 2 * (i - 4) + u)


def slot_groups(i):
    lo = 1 - i % 2
    slots = list(range(lo, lo + i + 1))
    return [slots[:4], slots[4:]] if len(slots) > 4 else [slots]


def build(nc, x, vec, units, conv_pw, pool_bd, final_g, out):
    qk_dram = nc.dram_tensor("qk_scratch", [PAIRS, 2, P, 2, S], F32).ap()
    v_dram = nc.dram_tensor("v_scratch", [TT, P, HEADS, 2 * DH], F32).ap()
    mix_dram = nc.dram_tensor("mix_scratch", [KT, P, S], F32).ap()
    x_tiles = x.rearrange("b (t p) d -> p (b t) d", p=P)
    out_tiles = out.rearrange("b (t p) d -> (b t) p d", p=P)

    with ExitStack() as ctx:
        def sem(name):
            return ctx.enter_context(nc.semaphore(name))

        def sb(where, name, shape, dt=F32):
            return where.enter_context(nc.sbuf_tensor(name, shape, dt))

        psum = ctx.enter_context(nc.psum_tensor("psum", [P, 8, CH], F32))
        bank = [psum[:, b, :] for b in range(8)]

        act_hi = sb(ctx, "act_hi", [P, KT, S], F32R)
        act_lo = sb(ctx, "act_lo", [P, KT, S], F32R)
        stage = sb(ctx, "stage", [P, UW])
        w_hi = [sb(ctx, f"w_hi{s}", [P, KT, UC], F32R) for s in range(2)]
        w_lo = [sb(ctx, f"w_lo{s}", [P, KT, UC], F32R) for s in range(2)]
        ident = sb(ctx, "ident", [P, P])
        vecs = sb(ctx, "vecs", [P, NVEC])
        ss = sb(ctx, "ss", [P, TT])
        var = sb(ctx, "var", [P, TT])
        root = sb(ctx, "root", [P, TT])
        tmp = sb(ctx, "tmp", [P, TT])
        rstd = sb(ctx, "rstd", [P, TT])

        with ExitStack() as mixers:
            nat = sb(mixers, "nat", [P, 2, 2, CH], F32R)
            ident_r = sb(mixers, "ident_r", [P, P], F32R)
            mask = sb(mixers, "mask", [P, 3 * P], F32R)
            with ExitStack() as norm_x:
                xt = sb(norm_x, "xt", [P, TT, D])
            with ExitStack() as first:
                ones_r = sb(first, "ones_r", [P, P], F32R)
                sig_gate = sb(first, "sig_gate", [P, 2, S])
                conv_u = sb(first, "conv_u", [P, 2, CONV_K - 1 + S])
                conv_acc = sb(first, "conv_acc", [P, 2, S])
                pool_in = sb(first, "pool_in", [P, 2, PAD + S])
                win_a = sb(first, "win_a", [P, 2, PAD + S])
                win_b = sb(first, "win_b", [P, 2, PAD + S])
                mm_hi = sb(first, "mm_hi", [P, 2, S], F32R)
                mm_lo = sb(first, "mm_lo", [P, 2, S], F32R)
                ln_root = sb(first, "ln_root", [P, S])
                ln_rstd = sb(first, "ln_rstd", [P, S])
                v_nat = sb(first, "v_nat", [P, 2, 4, 2, DH], F32R)
                pw_f = sb(first, "pw_f", [P, 2, D_CONV])
                pw_hi = sb(first, "pw_hi", [P, 2, D_CONV], F32R)
                pw_lo = sb(first, "pw_lo", [P, 2, D_CONV], F32R)
                pb_f = sb(first, "pb_f", [P, 2, P])
                pb_hi = sb(first, "pb_hi", [P, 2, P], F32R)
                pb_lo = sb(first, "pb_lo", [P, 2, P], F32R)
            with ExitStack() as attention:
                qs = [sb(attention, f"qs{a}", [P, S], F32R) for a in range(2)]
                ks = [sb(attention, f"ks{a}", [P, 2, S], F32R) for a in range(2)]
                vs = [sb(attention, f"vs{a}", [P, TT, 2 * DH], F32R) for a in range(2)]
                take = sb(attention, "take", [P, 2, S])
                keep = sb(attention, "keep", [P, 2, S])
                at_hi = sb(attention, "at_hi", [P, 2, TT, 2 * P], F32R)
                at_lo = sb(attention, "at_lo", [P, 2, TT, 2 * P], F32R)
                low_half = sb(attention, "low_half", [P, 2 * P])
                mix_pair = sb(attention, "mix_pair", [P, S])
        with ExitStack() as ffn:
            x1 = sb(ffn, "x1", [P, TT, D])
            xs = sb(ffn, "xs", [P, 4, D])
            wd_hi = sb(ffn, "wd_hi", [P, 2, D], F32R)
            wd_lo = sb(ffn, "wd_lo", [P, 2, D], F32R)
            inner_hi = sb(ffn, "inner_hi", [P, 2, S], F32R)
            inner_lo = sb(ffn, "inner_lo", [P, 2, S], F32R)
            gate_rows = sb(ffn, "gate_rows", [P, 2, 2 + S])
            hidden = sb(ffn, "hidden", [P, 2, S])
            fg = sb(ffn, "fg", [P, D])

        names = """consts_loaded small_loaded const_set masks_ready squared var_ready root_ready act_step dve_step
            pool_step rows_scaled tr_ready norm_hi norm_lo stage_loaded split_hi split_lo job_ready
            small_hi small_lo padded conv_rows conv_tap pool_mean pool_hi pool_lo pool_mm pool_out
            ln_hi ln_lo ln_sum ln_centred ln_sq_hi ln_sq_lo ln_var ln_var_eps ln_rooted ln_scaled ln_affine
            swish_done swish_hi swish_lo pw_mm pw_out mix_written v_hi nat_hi nat_lo first_over
            scores_ready scores_read stick_done tr_at_ready at_hi_done at_lo_done av_done low_copied
            mix_added mix7_hi mix7_lo x1_added
            gate_ready gate_copied gate_conv gelu_done val_ready gated inner_hi_done inner_lo_done down_ready
            down_added fg_loaded out_ready""".split()
        s = {n: sem(n) for n in names}
        x_loaded = [sem(f"x_loaded{q}") for q in range(4)]
        x_again = [sem(f"x_again{q}") for q in range(4)]
        out_written = [sem(f"out_written{q}") for q in range(4)]
        job_read = [sem(f"job_read{b}") for b in range(4)]
        nat_written = [sem(f"nat_written{b}") for b in range(2)]
        v_written = [sem(f"v_written{b}") for b in range(2)]
        qk_loaded = [sem(f"qk_loaded{a}") for a in range(2)]
        v_loaded = [sem(f"v_loaded{a}") for a in range(2)]

        def vcol(name, n=0, k=1):
            return vecs[:, VEC[name] + n:VEC[name] + n + k]

        def ffn_col(name, g, i, k, per):
            if isinstance(g, int):
                return vcol(name, (2 * g + i) * per + k)
            return vecs[:, bass.ds(g * (2 * per) + (VEC[name] + i * per + k), 1)]

        class Own:

            def __init__(self, eng, name):
                self.eng, self.sem, self.base, self.n = eng, s[name], 0, 0

            def done(self, ins):
                self.mark(ins)
                self.wait()

            def mark(self, ins):
                ins.then_inc(self.sem, 1)
                self.n += 1
                return self.n

            def wait(self, back=0):
                self.eng.wait_ge(self.sem, self.base + self.n - back)

            def enter(self, turn, per):
                self.outer, self.per = self.base + self.n, per
                self.base, self.n = turn * per + self.outer, 0

            def leave(self, turns):
                assert self.n == self.per, (self.n, self.per)
                self.base, self.n = self.outer + turns * self.per, 0

        block = ctx.enter_context(nc.Block())

        @block.sync
        def _(sp):
            def load_unit(j, unit):
                sp.wait_ge(s["split_lo"], j)
                sp.dma_start(stage[:], units[unit]).then_inc(s["stage_loaded"], 16)

            sp.dma_start(vecs[:], vec).then_inc(s["consts_loaded"], 16)
            for q in range(2):
                sp.dma_start(xt[:, 2 * q:2 * q + 2, :], x_tiles[:, 2 * q:2 * q + 2, :]).then_inc(x_loaded[q], 16)
            sp.dma_start(stage[:], units[0]).then_inc(s["stage_loaded"], 16)
            for q in range(2, 4):
                sp.dma_start(xt[:, 2 * q:2 * q + 2, :], x_tiles[:, 2 * q:2 * q + 2, :]).then_inc(x_loaded[q], 16)
            load_unit(1, 1)
            sp.wait_ge(s["norm_lo"], 2 * KT)
            sp.dma_start(pw_f[:], conv_pw).then_inc(s["small_loaded"], 16)
            sp.dma_start(pb_f[:], pool_bd).then_inc(s["small_loaded"], 16)
            for j in range(2, U_QK + 2):
                load_unit(j, j)

            def load_heads(pair, a):
                for b in range(2):
                    sp.wait_ge(nat_written[b], 16 * (2 * pair + 2))
                rows = slice(DH * a, DH * (a + 1))
                q_rows = qk_dram[pair, 0, rows, :, :]
                k_rows = qk_dram[pair, 1, rows, :, :]
                for hl in range(2):
                    part = slice(DH * hl, DH * (hl + 1))
                    sp.dma_start(qs[a][part, :].bitcast(F32), q_rows[:, hl, :]).then_inc(qk_loaded[a], 16)
                    sp.dma_start(ks[a][part, :, :].bitcast(F32), k_rows).then_inc(qk_loaded[a], 16)

            def load_values(pair, a):
                sp.dma_start(vs[a][:, :, :].bitcast(F32),
                             v_dram[:, :, 2 * pair + a, :].rearrange("t p c -> p t c")).then_inc(v_loaded[a], 16)

            sp.wait_ge(s["first_over"], 1)
            for b in range(2):
                sp.wait_ge(v_written[b], 16 * TT)
            for a in range(2):
                load_heads(0, a)
                load_values(0, a)
            with sp.Fori(0, PAIRS - 1) as p:
                sp.wait_ge(s["split_lo"], p + (U_QK + 2))
                sp.dma_start(stage[:], units[p + (U_QK + 2)]).then_inc(s["stage_loaded"], 16)
                for a in range(2):
                    sp.wait_ge(s["scores_ready"], p * 24 + 12 * (a + 1))
                    load_heads(p + 1, a)
                    sp.wait_ge(s["av_done"], p * 8 + 4 * (a + 1) + 2)
                    load_values(p + 1, a)
            load_unit(U_OUT + 1, U_OUT + 1)
            for m in range(NMIXJ):
                n = 2 if m < NMIXJ - 1 else 1
                sp.wait_ge(s["mix_written"], 16 * (4 if m < 2 else 2 * m + n))
                sp.wait_ge(s["split_lo"], J_MIX + m)
                sp.dma_start(stage[:, 0:n * S].rearrange("p (n t) -> p n t", n=n),
                             mix_dram[2 * m:2 * m + n].rearrange("n p t -> p n t")).then_inc(s["stage_loaded"], 16)
            load_unit(J_OUT2, U_OUT + 2)
            sp.wait_ge(s["mix_added"], 8 * PAIRS + 1)
            sp.wait_ge(s["mix7_lo"], 1)
            for q in range(4):
                sp.dma_start(x1[:, 2 * q:2 * q + 2, :], x_tiles[:, 2 * q:2 * q + 2, :]).then_inc(x_again[q], 16)
            sp.dma_start(fg[:], final_g.to_broadcast((P, D))).then_inc(s["fg_loaded"], 16)
            load_unit(J_OUT2 + 1, U_OUT + 3)
            load_unit(J_FFN_GATE0, U_FFN_GATE0)
            load_unit(J_FFN_VAL0, U_FFN_VAL0)
            with sp.Fori(0, NG - 1) as g:
                for r in range(3):
                    sp.wait_ge(s["split_lo"], g * 3 + (J_FFN + r))
                    sp.dma_start(stage[:], units[g * 3 + (U_FFN + r)]).then_inc(s["stage_loaded"], 16)
            load_unit(J_DOWN_LAST, NUNITS - 1)
            for t in range(TT):
                sp.wait_ge(s["out_ready"], t + 1)
                sp.dma_start(out_tiles[t], xs[:, t % 4, :]).then_inc(out_written[t % 4], 16)
            for q in range(4):
                sp.wait_ge(out_written[q], 16 * (TT // 4))

        @block.gpsimd
        def _(pool):
            own = Own(pool, "pool_step")
            own.mark(nc.gpsimd.memset(ident[:], 0.0))
            own.mark(nc.gpsimd.memset(take[:, 0, 0:3 * P], 0.0))
            own.wait()
            own.done(nc.gpsimd.affine_select(out=ident[:], in_=ident[:], compare_op=ALU.not_equal, fill=1.0, base=0,
                                             pattern=[[-1, P]], channel_multiplier=1))
            own.done(nc.gpsimd.affine_select(out=take[:, 0, P:2 * P], in_=take[:, 0, P:2 * P], compare_op=ALU.is_gt,
                                             fill=MASK, base=0, pattern=[[-1, P]], channel_multiplier=1))
            nc.gpsimd.tensor_copy(ident_r[:], ident[:]).then_inc(s["masks_ready"], 1)
            nc.gpsimd.tensor_copy(mask[:], take[:, 0, 0:3 * P]).then_inc(s["masks_ready"], 1)

            for name, banks in (("scores_read", 3), ("at_lo_done", 2), ("av_done", 2), ("gate_copied", 2), ("gated", 2),
                                ("down_added", 4), ("tr_at_ready", 1), ("mix_added", 1),
                                ("down_ready", 1)):
                pool.sem_inc(s[name], banks)

            pool.wait_ge(s["norm_lo"], 2 * KT)
            pool.wait_ge(s["masks_ready"], 2)
            nc.gpsimd.memset(conv_u[:, :, 0:CONV_K - 1], 0.0).then_inc(s["padded"], 1)
            own.mark(nc.gpsimd.memset(pool_in[:, :, 0:PAD], 0.0))
            own.mark(nc.gpsimd.memset(win_a[:, :, 0:PAD], 0.0))
            own.mark(nc.gpsimd.memset(win_b[:, :, 0:PAD], 0.0))
            nc.gpsimd.memset(ones_r[:].bitcast(F32), 1.0).then_inc(s["padded"], 1)
            own.wait()
            for b in range(4):
                pool.wait_ge(job_read[b], 3)

            def shifted_sum(dst, src, part, i, lag):
                t0 = PAD
                own.done(nc.gpsimd.tensor_tensor(dst[part, i, t0:t0 + S], src[part, i, t0:t0 + S],
                                                 src[part, i, t0 - lag:t0 - lag + S], ALU.add))
            every, upper = slice(0, P), slice(DH, P)
            shifted_sum(win_a, pool_in, every, 0, 1)
            shifted_sum(win_a, pool_in, every, 1, 1)
            shifted_sum(win_b, win_a, upper, 0, 2)
            shifted_sum(win_b, win_a, every, 1, 2)
            shifted_sum(win_a, win_b, every, 1, 4)
            shifted_sum(win_b, win_a, upper, 1, 8)
            for i in range(2):
                own.done(nc.gpsimd.tensor_copy(win_a[upper, i, PAD:], win_b[upper, i, PAD:]))
            for i in range(2):
                own.done(nc.gpsimd.tensor_tensor(win_a[:, i, PAD:2 * PAD], win_a[:, i, PAD:2 * PAD],
                                                 vcol("count_fix", PAD * i, PAD), ALU.mult))
                own.done(nc.gpsimd.tensor_scalar(win_a[:, i, PAD:], win_a[:, i, PAD:], vcol("inv_win", i), None,
                                                 ALU.mult))
                nc.gpsimd.tensor_tensor(win_b[:, i, PAD:], win_a[:, i, PAD:], pool_in[:, i, PAD:],
                                        ALU.subtract).then_inc(s["pool_mean"], 1)
            pool.wait_ge(s["pool_hi"], 2)
            for i in range(2):
                nc.gpsimd.tensor_tensor(mm_lo[:, i, :], win_b[:, i, PAD:], mm_hi[:, i, :].bitcast(F32),
                                        ALU.subtract).then_inc(s["pool_lo"], 1)

            def write_rows(pair, q):
                pool.wait_ge(s["nat_lo"], pair * 4 + (q + 1))
                pool.dma_start(qk_dram[pair, q % 2, :, :, (q // 2) * CH:(q // 2 + 1) * CH],
                               nat[:, q % 2].bitcast(F32)).then_inc(nat_written[q % 2], 16)

            pool.wait_ge(s["pool_out"], 4)
            for i in range(2):
                pool.dma_start(mix_dram[2 + i], pool_in[:, i, PAD:]).then_inc(s["mix_written"], 16)
            for q in range(4):
                write_rows(0, q)
            pool.wait_ge(s["pw_out"], 4)
            for i in range(2):
                pool.dma_start(mix_dram[i], sig_gate[:, i, :]).then_inc(s["mix_written"], 16)
            pool.wait_ge(s["mix_written"], 64)
            for b in range(2):
                pool.wait_ge(v_written[b], 16 * TT)
            nc.gpsimd.memset(at_hi[:, :, 0, 0:P].bitcast(F32), 0.0).then_inc(s["const_set"], 1)
            nc.gpsimd.memset(at_lo[:, :, 0, 0:P].bitcast(F32), 0.0).then_inc(s["const_set"], 1)
            pool.wait_ge(s["const_set"], 2)
            nc.gpsimd.memset(low_half[:], 0.0).then_inc(s["first_over"], 1)
            with pool.Fori(0, PAIRS - 1) as p:
                for q in range(4):
                    write_rows(p + 1, q)
                pool.wait_ge(s["mix_added"], p * 8 + 9)
                pool.dma_start(mix_dram[p + 4], mix_pair[:]).then_inc(s["mix_written"], 16)
            pool.wait_ge(s["mix_added"], 8 * PAIRS + 1)
            pool.wait_ge(s["mix7_lo"], 1)
            nc.gpsimd.memset(gate_rows[:, :, 0:2], 0.0).then_inc(s["const_set"], 1)

        @block.tensor
        def _(pe):
            def norm_transposes(r, h):
                src = xt if r == 0 else xs
                pe.wait_ge(s["rows_scaled"], 8 * r + 4 * h + 4)
                for k in range(KT):
                    n = 16 * r + 8 * h + k
                    if n % 16 >= 4:
                        pe.wait_ge(s["norm_lo"], n - 3)
                    for q in range(4):
                        last = nc.tensor.transpose(bank[4 * r + k % 4][:, q * P:(q + 1) * P],
                                                   src[:, (4 * h if r == 0 else 0) + q, k * P:(k + 1) * P], ident[:])
                    last.then_inc(s["tr_ready"], 1)

            def products(out, w, a, k, first, last):
                for n, (lhs, rhs) in enumerate(((w[0], a[0]), (w[0], a[1]), (w[1], a[0]))):
                    ins = nc.tensor.matmul(out, lhs, rhs, start=(first and n == 0), stop=(last and n == 2))
                return ins

            def weight_pair(slot, k, i):
                return [w[slot][:, k, i * P:(i + 1) * P] for w in (w_hi, w_lo)]

            def act_pair(k, c):
                return [t[:, k, c * CH:(c + 1) * CH] for t in (act_hi, act_lo)]

            def project(out, slot, q):
                for k in range(KT):
                    ins = products(out, weight_pair(slot, k, q % 2), act_pair(k, q // 2), k, k == 0, k == KT - 1)
                return ins

            def token_rows(out, slot, t):
                for k in range(KT):
                    a = [x_[:, k, t * P:(t + 1) * P] for x_ in (act_hi, act_lo)]
                    w = [w_[slot][:, k, :] for w_ in (w_hi, w_lo)]
                    ins = products(out, a, w, k, k == 0, k == KT - 1)
                return ins

            pe.wait_ge(s["masks_ready"], 2)
            norm_transposes(0, 0)
            norm_transposes(0, 1)
            for j in range(PJ_LOOP):
                unit, q = (j // 4, j % 4) if j < 12 else (U_V0 + (j - 12) // TT, (j - 12) % TT)
                if j >= PJ_QK0:
                    unit, q = U_QK, j - PJ_QK0
                if q == 0:
                    pe.wait_ge(s["split_lo"], unit + 1)
                if j == 0:
                    pe.wait_ge(s["norm_lo"], 2 * KT)
                if j >= 4:
                    pe.wait_ge(job_read[j % 4], j // 4)
                if unit in (U_V0, U_V1):
                    ins = token_rows(bank[j % 4][:, 0:UC], unit % 2, q)
                else:
                    ins = project(bank[j % 4][:], unit % 2, q)
                ins.then_inc(s["job_ready"], 1)
                if j == PJ_POOL_MM:
                    pe.wait_ge(s["pool_lo"], 2)
                    pe.wait_ge(s["small_lo"], 2)
                    for n in range(4):
                        i, c = n % 2, n // 2
                        ins = products(bank[4 + n][:], (pb_hi[:, i, :], pb_lo[:, i, :]),
                                       [m[:, i, c * CH:(c + 1) * CH] for m in (mm_hi, mm_lo)], 0, True, True)
                        ins.then_inc(s["pool_mm"], 1)

            def channel_sums(b0, name):
                for c in range(2):
                    for n in range(4):
                        src = (mm_hi, mm_lo)[n % 2]
                        ins = nc.tensor.matmul(bank[b0 + c][:], ones_r[:], src[:, n // 2, c * CH:(c + 1) * CH],
                                               start=(n == 0), stop=(n == 3))
                    ins.then_inc(s[name], 1)

            pe.wait_ge(s["ln_lo"], 2)
            pe.wait_ge(s["pool_out"], 4)
            pe.wait_ge(s["padded"], 2)
            channel_sums(4, "ln_sum")
            pe.wait_ge(s["ln_sq_lo"], 2)
            channel_sums(6, "ln_var")
            pe.wait_ge(s["swish_lo"], 2)
            for n in range(4):
                m, c = n % 2, n // 2
                for k in range(2):
                    ins = products(bank[4 + n][:], [w[:, k, m * P:(m + 1) * P] for w in (pw_hi, pw_lo)],
                                   [t[:, k, c * CH:(c + 1) * CH] for t in (mm_hi, mm_lo)], k, k == 0, k == 1)
                ins.then_inc(s["pw_mm"], 1)

            def scores(p, a, i):
                if i == 0:
                    pe.wait_ge(qk_loaded[a], p * 64 + 64)
                for u, (c0, n) in enumerate(score_units(i)):
                    idx = unit_index(a, i, u)
                    pe.wait_ge(s["scores_read"], p * 24 + (idx + 1))
                    out = bank[idx % 3]
                    for hl in range(2):
                        if hl == 1 and c0 + n == max(P * (i + 1), 256):
                            m0 = P if i == 0 else 0
                            nc.tensor.matmul(out[:, n - 256:n], ident_r[:], mask[:, m0:m0 + 256],
                                             start=False, stop=False)
                        ins = nc.tensor.matmul(out[:, 0:n], qs[a][:, i * P:(i + 1) * P], ks[a][:, hl, c0:c0 + n],
                                               start=(hl == 0), stop=(hl == 1))
                    ins.then_inc(s["scores_ready"], 1)

            def weight_transposes(p, a, i):
                st = 8 * a + i
                pe.wait_ge(s["stick_done"], p * 16 + (st + 1))
                for u, slots in enumerate(slot_groups(i)):
                    idx = unit_index(a, i, u)
                    pe.wait_ge(s["at_lo_done"], p * 24 + (idx + 1))
                    for n, slot in enumerate(slots):
                        b = 2 * (i // 2) + 1 - slot
                        ins = nc.tensor.transpose(bank[3 + idx % 2][:, n * P:(n + 1) * P],
                                                  take[:, st % 2, b * P:(b + 1) * P], ident[:])
                    ins.then_inc(s["tr_at_ready"], 1)

            def values(p, a, j):
                c = 4 * a + j
                if j == 0:
                    pe.wait_ge(v_loaded[a], p * 16 + 16)
                pe.wait_ge(s["at_lo_done"], p * 24 + (unit_index(a, 2 * j + 1, len(slot_groups(2 * j + 1)) - 1) + 3))
                pe.wait_ge(s["mix_added"], p * 8 + (c + 1))
                for slot in range(2 * j + 2):
                    for t in (at_hi, at_lo):
                        ins = nc.tensor.matmul(bank[5][:, 0:2 * P], vs[a][:, 2 * j + 1 - slot, :], t[:, j % 2, slot, :],
                                               start=(slot == 0 and t is at_hi),
                                               stop=(slot == 2 * j + 1 and t is at_lo))
                ins.then_inc(s["av_done"], 1)

            def next_rows(p, st):
                q, third = st // 3, st % 3
                if st == 0:
                    pe.wait_ge(s["split_lo"], p + (U_QK + 2))
                if third == 0:
                    pe.wait_ge(s["nat_lo"], p * 4 + (4 + q - 1))
                for m in range(8 * third, 8 * third + 8):
                    k, n = m // 3, m % 3
                    w, t = weight_pair(0, k, q % 2), act_pair(k, q // 2)
                    ins = nc.tensor.matmul(bank[6 + q % 2][:], w[n // 2], t[n % 2], start=(m == 0), stop=(m == 23))
                if third == 2:
                    ins.then_inc(s["job_ready"], 1)

            def attend(p, more):
                scores(p, 0, 0)
                scores(p, 0, 1)
                for st in range(16):
                    if st + 2 < 16:
                        scores(p, (st + 2) // 8, (st + 2) % 8)
                    if more and st < 12:
                        next_rows(p, st)
                    weight_transposes(p, st // 8, st % 8)
                    if st % 2 == 0 and st > 0:
                        values(p, (st - 1) // 8, (st - 1) % 8 // 2)
                values(p, 1, 3)

            pe.wait_ge(s["pw_out"], 4)
            with pe.Fori(0, PAIRS - 1) as p:
                attend(p, True)
            attend(PAIRS - 1, False)

            pe.wait_ge(s["mix7_lo"], 1)
            for m in range(4 * TT):
                n, t = m // TT, m % TT
                if t == 0:
                    pe.wait_ge(s["split_lo"], (U_OUT + n if n < 2 else J_OUT2 + n - 2) + 1)
                    if n == 0:
                        pe.wait_ge(s["split_lo"], J_OUT2)
                if m >= 4:
                    pe.wait_ge(s["x1_added"], m - 3)
                token_rows(bank[m % 4][:, 0:UC], n % 2, t).then_inc(s["job_ready"], 1)
            norm_transposes(1, 0)
            norm_transposes(1, 1)

            def gate(g, job, after_norm=False):
                pe.wait_ge(s["split_lo"], job + 1)
                for q in range(4):
                    if after_norm and q % 2 == 0:
                        pe.wait_ge(s["norm_lo"], 16 + 8 * (q // 2) + 8)
                    pe.wait_ge(s["gate_copied"], g * 4 + (q + 1))
                    project(bank[q % 2][:], 0, q).then_inc(s["gate_ready"], 1)

            def val(g):
                pe.wait_ge(s["split_lo"], g * 3 + (J_FFN_VAL0 + 1))
                for q in range(4):
                    pe.wait_ge(s["gated"], g * 4 + (q + 1))
                    project(bank[2 + q % 2][:], 1, q).then_inc(s["val_ready"], 1)

            def down(g, unit_job):
                pe.wait_ge(s["split_lo"], unit_job + 1)
                pe.wait_ge(s["inner_lo_done"], g * 4 + 4)
                for m in range(2 * TT):
                    t, n = m // 2, m % 2
                    pe.wait_ge(s["down_added"], g * 16 + (m + 1))
                    for i in range(2):
                        ins = products(bank[4 + m % 4][:], [x_[:, i, t * P:(t + 1) * P] for x_ in (inner_hi, inner_lo)],
                                       [w[:, i, n * CH:(n + 1) * CH] for w in (wd_hi, wd_lo)], i, i == 0, i == 1)
                    ins.then_inc(s["down_ready"], 1)

            gate(0, J_FFN_GATE0, after_norm=True)
            val(0)
            with pe.Fori(1, NG) as g:
                gate(g, g * 3 + (J_FFN - 3))
                down(g - 1, g * 3 + (J_FFN - 2))
                val(g)
            down(NG - 1, J_DOWN_LAST)

        @block.scalar
        def _(act):
            own = Own(act, "act_step")

            def squares(r, h, src):
                for q in range(4):
                    t = 4 * h + q
                    if r == 0:
                        act.wait_ge(x_loaded[t // 2], 16)
                        unused = psum[:, 4 + 2 * (q % 2):6 + 2 * (q % 2), :]
                    elif r == 1:
                        act.wait_ge(s["x1_added"], 3 * TT + t + 1)
                        act.wait_ge(s["tr_ready"], 16 + 8 * h)
                        unused = xs[:, q, :]
                    else:
                        act.wait_ge(s["down_added"], 16 * (NG - 1) + 2 * t + 2 + 4)
                        unused = psum[:, 2 * (q % 2):2 + 2 * (q % 2), :]
                    if r != 1 and q + 4 * h >= 2:
                        act.wait_ge(s["squared"], 8 * r + 4 * h + q - 1)
                    nc.scalar.activation(unused, src[:, t, :], ACT.Square,
                                         accum_out=ss[:, t:t + 1]).then_inc(s["squared"], 1)
                act.wait_ge(s["var_ready"], 2 * r + h + 1)
                nc.scalar.activation(root[:, 4 * h:4 * h + 4], var[:, 4 * h:4 * h + 4],
                                     ACT.Sqrt).then_inc(s["root_ready"], 1)

            def norm_high(r, h, gain):
                for k in range(KT):
                    act.wait_ge(s["tr_ready"], 16 * r + 8 * h + k + 1)
                    nc.scalar.activation(act_hi[:, k, h * CH:(h + 1) * CH], bank[4 * r + k % 4], ACT.Copy,
                                         scale=vcol(gain, k)).then_inc(s["norm_hi"], 1)

            def split_high(job, dst, src=None):
                act.wait_ge(s["stage_loaded"], job * 16 + 16)
                nc.scalar.activation(dst, stage[:] if src is None else src, ACT.Copy).then_inc(s["split_hi"], 1)

            def flat(t):
                return t[:].rearrange("p k n -> p (k n)")

            act.wait_ge(s["consts_loaded"], 16)
            squares(0, 0, xt)
            norm_high(0, 0, "g1")
            split_high(0, flat(w_hi[0]))
            squares(0, 1, xt)
            norm_high(0, 1, "g1")
            split_high(1, flat(w_hi[1]))
            act.wait_ge(s["small_loaded"], 32)
            nc.scalar.activation(pw_hi[:], pw_f[:], ACT.Copy).then_inc(s["small_hi"], 1)
            nc.scalar.activation(pb_hi[:], pb_f[:], ACT.Copy).then_inc(s["small_hi"], 1)

            def job(j):
                act.wait_ge(s["job_ready"], j + 1)
                return bank[j % 4]

            for q in range(4):
                nc.scalar.activation(sig_gate[:, q % 2, (q // 2) * CH:(q // 2 + 1) * CH], job(q),
                                     ACT.Sigmoid).then_inc(job_read[q], 1)
            split_high(U_POOL, flat(w_hi[0]))
            act.wait_ge(s["job_ready"], 8)
            split_high(U_V0, flat(w_hi[1]))
            act.wait_ge(s["padded"], 2)
            for q in range(4):
                t0 = PAD + (q // 2) * CH
                nc.scalar.activation(pool_in[:, q % 2, t0:t0 + CH], job(8 + q), ACT.Copy).then_inc(job_read[q], 1)
            split_high(U_V1, flat(w_hi[0]))

            def write_values(n):
                j = 12 + n
                act.wait_ge(job_read[j % 4], j // 4 + 1)
                half, t = n // TT, n % TT
                act.dma_start(v_dram[t, :, 4 * half:4 * half + 4, :],
                              v_nat[:, n % 2].rearrange("p h l c -> p h (l c)").bitcast(F32)
                              ).then_inc(v_written[n % 2], 16)

            for n in range(2 * TT):
                j = 12 + n
                act.wait_ge(s["job_ready"], j + 1)
                if n >= 2:
                    act.wait_ge(v_written[n % 2], 16 * (n // 2))
                nc.scalar.activation(v_nat[:, n % 2, :, 0, :], bank[j % 4][:, 0:UC].rearrange("p (h c) -> p h c", h=4),
                                     ACT.Copy).then_inc(s["v_hi"], 1)
                if n > 0:
                    write_values(n - 1)
                if n == TT - 1:
                    split_high(U_QK, flat(w_hi[1]))
                    act.wait_ge(s["pool_mean"], 2)
                    for i in range(2):
                        nc.scalar.activation(mm_hi[:, i, :], win_b[:, i, PAD:], ACT.Copy).then_inc(s["pool_hi"], 1)
                if j == PJ_POOL_MM:
                    for m in range(4):
                        act.wait_ge(s["pool_mm"], m + 1)
                        i, t0 = m % 2, PAD + (m // 2) * CH
                        nc.scalar.activation(pool_in[:, i, t0:t0 + CH], bank[4 + m], ACT.Copy,
                                             scale=vcol("pool_scale", i)).then_inc(s["pool_out"], 1)
            write_values(2 * TT - 1)
            split_high(U_QK + 1, flat(w_hi[0]))

            def rows_high(pair, q):
                act.wait_ge(s["job_ready"], pair * 4 + (PJ_QK0 + q + 1))
                act.wait_ge(nat_written[q % 2], pair * 32 + 16 * (q // 2))
                src = bank[q] if isinstance(pair, int) and pair == 0 else bank[6 + q % 2]
                nc.scalar.activation(nat[:, q % 2, 0, :], src, ACT.Copy).then_inc(s["nat_hi"], 1)

            for q in range(4):
                rows_high(0, q)

            for i in range(2):
                act.wait_ge(s["conv_tap"], 2 * CONV_K - 1 + i)
                nc.scalar.activation(mm_hi[:, i, :], conv_acc[:, i, :], ACT.Copy).then_inc(s["ln_hi"], 1)
            for i in range(2):
                act.wait_ge(s["ln_centred"], 4)
                own.done(nc.scalar.activation(sig_gate[:, i, :], conv_acc[:, i, :], ACT.Square))
                nc.scalar.activation(mm_hi[:, i, :], sig_gate[:, i, :], ACT.Copy).then_inc(s["ln_sq_hi"], 1)
            for c in range(2):
                act.wait_ge(s["ln_var_eps"], c + 1)
                nc.scalar.activation(ln_root[:, c * CH:(c + 1) * CH], ln_rstd[:, c * CH:(c + 1) * CH],
                                     ACT.Sqrt).then_inc(s["ln_rooted"], 1)
            for i in range(2):
                act.wait_ge(s["ln_scaled"], i + 1)
                nc.scalar.activation(sig_gate[:, i, :], conv_acc[:, i, :], ACT.Identity, scale=vcol("ln_g", i),
                                     bias=vcol("ln_b", i)).then_inc(s["ln_affine"], 1)
                nc.scalar.activation(conv_u[:, i, 0:S], conv_acc[:, i, :], ACT.Sigmoid, scale=vcol("ln_g", i),
                                     bias=vcol("ln_b", i)).then_inc(s["ln_affine"], 1)
            for i in range(2):
                act.wait_ge(s["swish_done"], i + 1)
                nc.scalar.activation(mm_hi[:, i, :], conv_acc[:, i, :], ACT.Copy).then_inc(s["swish_hi"], 1)
            for n in range(4):
                act.wait_ge(s["pw_mm"], n + 1)
                nc.scalar.activation(sig_gate[:, n % 2, (n // 2) * CH:(n // 2 + 1) * CH], bank[4 + n], ACT.Identity,
                                     bias=vcol("pw_b", n % 2)).then_inc(s["pw_out"], 1)

            act.wait_ge(s["first_over"], 1)

            def squeeze(p, st):
                a, i = st // 8, st % 8
                act.wait_ge(s["tr_at_ready"],
                            p * 24 + (1 if st < 2 else unit_index((st - 2) // 8, (st - 2) % 8,
                                                                  len(slot_groups((st - 2) % 8)) - 1) + 2))
                for u, (c0, n) in enumerate(score_units(i)):
                    idx = unit_index(a, i, u)
                    n = min(n, P * (i + 1) - c0)
                    act.wait_ge(s["scores_ready"], p * 24 + (idx + 1))
                    nc.scalar.activation(take[:, st % 2, c0:c0 + n], bank[idx % 3][:, 0:n], ACT.Sigmoid, scale=SCALE)
                    nc.scalar.activation(keep[:, st % 2, c0:c0 + n], bank[idx % 3][:, 0:n], ACT.Sigmoid,
                                         scale=-SCALE).then_inc(s["scores_read"], 1)

            def weights_high(p, st):
                a, i = st // 8, st % 8
                j = i // 2
                act.wait_ge(s["av_done"], p * 8 + (4 * a + j + 1))
                for u, slots in enumerate(slot_groups(i)):
                    idx = unit_index(a, i, u)
                    act.wait_ge(s["tr_at_ready"], p * 24 + (idx + 2))
                    nc.scalar.activation(at_hi[:, j % 2, slots[0]:slots[-1] + 1, (i % 2) * P:(i % 2 + 1) * P],
                                         bank[3 + idx % 2][:, 0:P * len(slots)].rearrange("p (s t) -> p s t", t=P),
                                         ACT.Copy).then_inc(s["at_hi_done"], 1)

            def copy_low(p, c):
                a = c // 4
                act.wait_ge(s["av_done"], p * 8 + (c + 3))
                act.wait_ge(s["mix_added"], p * 8 + (c + 1))
                nc.scalar.activation(low_half[DH * a:DH * (a + 1), :], bank[5][DH:P, 0:2 * P],
                                     ACT.Copy).then_inc(s["low_copied"], 1)

            def mix_high(m):
                n = 2 if m < NMIXJ - 1 else 1
                split_high(J_MIX + m, act_hi[:, 2 * m:2 * m + n, :],
                           stage[:, 0:n * S].rearrange("p (n t) -> p n t", n=n))

            def attend(p, more):
                squeeze(p, 0)
                for st in range(16):
                    if st + 1 < 16:
                        squeeze(p, st + 1)
                    if more and st % 3 == 2 and st < 12:
                        rows_high(p + 1, st // 3)
                    if more and st == 13:
                        split_high(p + (U_QK + 2), flat(w_hi[0]))
                    if not more and st == 1:
                        split_high(U_OUT + 1, flat(w_hi[1]))
                    if not more and st % 3 == 1 and st > 1:
                        mix_high(st // 3 - 1)
                    weights_high(p, st)
                    if st % 2 == 1 and st > 1:
                        copy_low(p, (st - 3) // 2)
                copy_low(p, 7)

            with act.Fori(0, PAIRS - 1) as p:
                attend(p, True)
            attend(PAIRS - 1, False)
            act.wait_ge(s["mix_added"], 8 * PAIRS + 1)
            nc.scalar.activation(act_hi[:, KT - 1, :], mix_pair[:], ACT.Copy).then_inc(s["mix7_hi"], 1)

            act.wait_ge(s["job_ready"], PJ_OUT + TT)
            split_high(J_OUT2, flat(w_hi[0]))
            act.wait_ge(s["job_ready"], PJ_OUT + 2 * TT)
            split_high(J_OUT2 + 1, flat(w_hi[1]))
            act.wait_ge(s["job_ready"], PJ_OUT + 3 * TT)
            split_high(J_FFN_GATE0, flat(w_hi[0]))
            squares(1, 0, x1)
            norm_high(1, 0, "g2")
            squares(1, 1, x1)
            norm_high(1, 1, "g2")
            split_high(J_FFN_VAL0, flat(w_hi[1]))

            def ffn(g, more):
                for q in range(4):
                    act.wait_ge(s["gate_ready"], g * 4 + (q + 1))
                    t0 = 2 + (q // 2) * CH
                    nc.scalar.activation(gate_rows[:, q % 2, t0:t0 + CH], bank[q % 2],
                                         ACT.Copy).then_inc(s["gate_copied"], 1)
                if more:
                    split_high(g * 3 + J_FFN, flat(w_hi[0]))
                for q in range(4):
                    act.wait_ge(s["gate_conv"], g * 4 + (q + 1))
                    h = hidden[:, q % 2, (q // 2) * CH:(q // 2 + 1) * CH]
                    nc.scalar.activation(h, h, ACT.Gelu).then_inc(s["gelu_done"], 1)
                act.wait_ge(s["down_ready"], g * 16 + 1)
                split_high(g * 3 + (J_FFN + 1) if more else J_DOWN_LAST, flat(wd_hi))
                for q in range(4):
                    act.wait_ge(s["gated"], g * 4 + (q + 3))
                    c = slice((q // 2) * CH, (q // 2 + 1) * CH)
                    nc.scalar.activation(inner_hi[:, q % 2, c], hidden[:, q % 2, c],
                                         ACT.Copy).then_inc(s["inner_hi_done"], 1)
                if more:
                    split_high(g * 3 + (J_FFN + 2), flat(w_hi[1]))

            with act.Fori(0, NG - 1) as g:
                ffn(g, True)
            ffn(NG - 1, False)
            squares(2, 0, x1)
            squares(2, 1, x1)

        @block.vector
        def _(dve):
            own = Own(dve, "dve_step")
            tsc, stt, tt = nc.vector.tensor_scalar, nc.vector.scalar_tensor_tensor, nc.vector.tensor_tensor

            def rsqrt(r, h):
                cols = slice(4 * h, 4 * h + 4)
                dve.wait_ge(s["squared"], 8 * r + 4 * h + 4)
                tsc(var[:, cols], ss[:, cols], 1.0 / D, EPS, ALU.mult, ALU.add).then_inc(s["var_ready"], 1)
                dve.wait_ge(s["root_ready"], 2 * r + h + 1)
                own.done(nc.vector.reciprocal(tmp[:, cols], root[:, cols]))
                own.done(tt(tmp[:, cols], tmp[:, cols], var[:, cols], ALU.mult))
                own.done(tt(tmp[:, cols], tmp[:, cols], root[:, cols], ALU.add))
                own.done(tsc(tmp[:, cols], tmp[:, cols], 0.5, None, ALU.mult))
                own.done(nc.vector.reciprocal(rstd[:, cols], tmp[:, cols]))

            def scale_rows(h, dst, src):
                for q in range(4):
                    t = 4 * h + q
                    tsc(dst(t), src[:, t, :], rstd[:, t:t + 1], None, ALU.mult).then_inc(s["rows_scaled"], 1)

            def norm_low(r, h, gain):
                for k in range(KT):
                    dve.wait_ge(s["norm_hi"], 16 * r + 8 * h + k + 1)
                    c = slice(h * CH, (h + 1) * CH)
                    stt(act_lo[:, k, c], bank[4 * r + k % 4], vcol(gain, k), act_hi[:, k, c].bitcast(F32),
                        ALU.mult, ALU.subtract).then_inc(s["norm_lo"], 1)

            def flat(t):
                return t[:].rearrange("p k n -> p (k n)")

            def split_low(job, lo, hi, src=None):
                dve.wait_ge(s["split_hi"], job + 1)
                tt(lo, stage[:] if src is None else src, hi.bitcast(F32), ALU.subtract).then_inc(s["split_lo"], 1)

            def split_unit_low(job, slot):
                split_low(job, flat(w_lo[slot]), flat(w_hi[slot]))

            dve.wait_ge(s["consts_loaded"], 16)
            for h in range(2):
                rsqrt(0, h)
                scale_rows(h, lambda t: xt[:, t, :], xt)
                norm_low(0, h, "g1")
                split_unit_low(h, h)
            for n, (f, hi, lo) in enumerate(((pw_f, pw_hi, pw_lo), (pb_f, pb_hi, pb_lo))):
                dve.wait_ge(s["small_hi"], n + 1)
                tt(lo[:], f[:], hi[:].bitcast(F32), ALU.subtract).then_inc(s["small_lo"], 1)
            split_unit_low(U_POOL, 0)

            dve.wait_ge(s["padded"], 1)
            for q in range(4):
                i, c = q % 2, q // 2
                dve.wait_ge(job_read[q], 1)
                dve.wait_ge(s["job_ready"], 4 + q + 1)
                tt(conv_u[:, i, CONV_K - 1 + c * CH:CONV_K - 1 + (c + 1) * CH], bank[q],
                   sig_gate[:, i, c * CH:(c + 1) * CH], ALU.mult).then_inc(job_read[q], 1)
            for q in range(4):
                dve.wait_ge(job_read[q], 2)

            def conv_taps(first, count):
                for n in range(first, first + count):
                    i, k = n % 2, n // 2
                    rows, w = conv_u[:, i, k:k + S], vcol("conv_w", i * CONV_K + k)
                    if k == 0:
                        ins = tsc(conv_acc[:, i, :], rows, w, vcol("conv_b", i), ALU.mult, ALU.add)
                    else:
                        dve.wait_ge(s["conv_tap"], n - 1)
                        ins = stt(conv_acc[:, i, :], rows, w, conv_acc[:, i, :], ALU.mult, ALU.add)
                    ins.then_inc(s["conv_tap"], 1)

            conv_taps(0, 2)
            split_unit_low(U_V0, 1)
            conv_taps(2, 14)
            split_unit_low(U_V1, 0)
            for n in range(2 * TT):
                j = 12 + n
                if n == TT:
                    split_unit_low(U_QK, 1)
                dve.wait_ge(s["v_hi"], n + 1)
                tt(v_nat[:, n % 2, :, 1, :], bank[j % 4][:, 0:UC].rearrange("p (h c) -> p h c", h=4),
                   v_nat[:, n % 2, :, 0, :].bitcast(F32), ALU.subtract).then_inc(job_read[j % 4], 1)
                conv_taps(16 + 2 * n, 2)
            split_unit_low(U_QK + 1, 0)

            def rows_low(pair, q):
                dve.wait_ge(s["nat_hi"], pair * 4 + (q + 1))
                src = bank[q] if isinstance(pair, int) and pair == 0 else bank[6 + q % 2]
                tt(nat[:, q % 2, 1, :], src, nat[:, q % 2, 0, :].bitcast(F32), ALU.subtract).then_inc(s["nat_lo"], 1)

            for q in range(4):
                rows_low(0, q)
                conv_taps(48 + 3 * q, 3)
            conv_taps(60, 2)

            def low_of(name_in, name_out, src):
                for i in range(2):
                    dve.wait_ge(s[name_in], i + 1)
                    tt(mm_lo[:, i, :], src[:, i, :], mm_hi[:, i, :].bitcast(F32), ALU.subtract).then_inc(s[name_out], 1)

            low_of("ln_hi", "ln_lo", conv_acc)
            for c in range(2):
                dve.wait_ge(s["ln_sum"], c + 1)
                for i in range(2):
                    a = conv_acc[:, i, c * CH:(c + 1) * CH]
                    stt(a, bank[4 + c], -1.0 / D_CONV, a, ALU.mult, ALU.add).then_inc(s["ln_centred"], 1)
            low_of("ln_sq_hi", "ln_sq_lo", sig_gate)
            for c in range(2):
                dve.wait_ge(s["ln_var"], c + 1)
                tsc(ln_rstd[:, c * CH:(c + 1) * CH], bank[6 + c], 1.0 / D_CONV, EPS, ALU.mult,
                    ALU.add).then_inc(s["ln_var_eps"], 1)
            dve.wait_ge(s["ln_rooted"], 2)
            own.done(nc.vector.reciprocal(ln_rstd[:], ln_root[:]))
            for i in range(2):
                tt(conv_acc[:, i, :], conv_acc[:, i, :], ln_rstd[:], ALU.mult).then_inc(s["ln_scaled"], 1)
            for i in range(2):
                dve.wait_ge(s["ln_affine"], 2 * i + 2)
                tt(conv_acc[:, i, :], sig_gate[:, i, :], conv_u[:, i, 0:S], ALU.mult).then_inc(s["swish_done"], 1)
            low_of("swish_hi", "swish_lo", conv_acc)

            def stick(p, st):
                a, i = st // 8, st % 8
                n = P * (i + 1)
                dve.wait_ge(s["scores_read"], p * 24 + (unit_index(a, i, len(score_units(i)) - 1) + 4))
                back = keep[:, st % 2, 0:n][:, ::-1]
                own.done(nc.vector.tensor_tensor_scan(back, back, back, 1.0, ALU.mult, ALU.bypass))
                tt(take[:, st % 2, 0:n - 1], take[:, st % 2, 0:n - 1], keep[:, st % 2, 1:n],
                   ALU.mult).then_inc(s["stick_done"], 1)

            def weights_low(p, st):
                a, i = st // 8, st % 8
                j = i // 2
                for u, slots in enumerate(slot_groups(i)):
                    idx = unit_index(a, i, u)
                    dve.wait_ge(s["at_hi_done"], p * 24 + (idx + 1))
                    where = (slice(None), j % 2, slice(slots[0], slots[-1] + 1), slice((i % 2) * P, (i % 2 + 1) * P))
                    tt(at_lo[where], bank[3 + idx % 2][:, 0:P * len(slots)].rearrange("p (s t) -> p s t", t=P),
                       at_hi[where].bitcast(F32), ALU.subtract).then_inc(s["at_lo_done"], 1)

            def add_low(p, c):
                a, j = c // 4, c % 4
                dve.wait_ge(s["low_copied"], p * 8 + (c + 1))
                if c == 0:
                    dve.wait_ge(s["mix_written"], p * 16 + 16 * 4)
                rows = slice(DH * a, DH * (a + 1))
                tt(mix_pair[rows, 2 * P * j:2 * P * (j + 1)], bank[5][0:DH, 0:2 * P], low_half[rows, :],
                   ALU.add).then_inc(s["mix_added"], 1)

            def mix_low(m):
                n = 2 if m < NMIXJ - 1 else 1
                split_low(J_MIX + m, act_lo[:, 2 * m:2 * m + n, :], act_hi[:, 2 * m:2 * m + n, :],
                          stage[:, 0:n * S].rearrange("p (n t) -> p n t", n=n))

            def attend(p, more):
                stick(p, 0)
                for st in range(16):
                    if st + 1 < 16:
                        stick(p, st + 1)
                    if more and st % 3 == 2 and st < 12:
                        rows_low(p + 1, st // 3)
                    if more and st == 13:
                        split_unit_low(p + (U_QK + 2), 0)
                    if not more and st == 1:
                        split_unit_low(U_OUT + 1, 1)
                    if not more and st % 3 == 1 and st > 1:
                        mix_low(st // 3 - 1)
                    weights_low(p, st)
                    if st % 2 == 1 and st > 1:
                        add_low(p, (st - 3) // 2)
                add_low(p, 7)

            dve.wait_ge(s["first_over"], 1)
            with dve.Fori(0, PAIRS - 1) as p:
                own.enter(p, 16)
                attend(p, True)
                own.leave(PAIRS - 1)
            attend(PAIRS - 1, False)
            dve.wait_ge(s["mix7_hi"], 1)
            tt(act_lo[:, KT - 1, :], mix_pair[:], act_hi[:, KT - 1, :].bitcast(F32), ALU.subtract).then_inc(s["mix7_lo"], 1)

            for m in range(4 * TT):
                n, t = m // TT, m % TT
                if m == TT:
                    split_unit_low(J_OUT2, 0)
                if m == 2 * TT:
                    split_unit_low(J_OUT2 + 1, 1)
                if m == 3 * TT:
                    split_unit_low(J_FFN_GATE0, 0)
                if n == 0 and t % 2 == 0:
                    dve.wait_ge(x_again[t // 2], 16)
                dve.wait_ge(s["job_ready"], PJ_OUT + m + 1)
                r = x1[:, t, n * UC:(n + 1) * UC]
                tt(r, bank[m % 4][:, 0:UC], r, ALU.add).then_inc(s["x1_added"], 1)
            for h in range(2):
                rsqrt(1, h)
                scale_rows(h, lambda t: xs[:, t % 4, :], x1)
                norm_low(1, h, "g2")
            split_unit_low(J_FFN_VAL0, 1)

            def ffn(g, more, down):
                for q in range(4):
                    i, c0 = q % 2, (q // 2) * CH
                    dve.wait_ge(s["gate_copied"], g * 4 + (q + 3))
                    h = hidden[:, i, c0:c0 + CH]
                    own.done(tsc(h, gate_rows[:, i, c0:c0 + CH], ffn_col("ffn_w", g, i, 0, 3),
                                 ffn_col("ffn_b", g, i, 0, 1), ALU.mult, ALU.add))
                    own.done(stt(h, gate_rows[:, i, c0 + 1:c0 + 1 + CH], ffn_col("ffn_w", g, i, 1, 3), h,
                                 ALU.mult, ALU.add))
                    stt(h, gate_rows[:, i, c0 + 2:c0 + 2 + CH], ffn_col("ffn_w", g, i, 2, 3), h,
                        ALU.mult, ALU.add).then_inc(s["gate_conv"], 1)
                if more:
                    split_unit_low(g * 3 + J_FFN, 0)
                if down:
                    add_down(g - 1)
                split_low(g * 3 + (J_FFN + 1) if more else J_DOWN_LAST, flat(wd_lo), flat(wd_hi))
                for q in range(4):
                    i, c = q % 2, slice((q // 2) * CH, (q // 2 + 1) * CH)
                    dve.wait_ge(s["gelu_done"], g * 4 + (q + 1))
                    dve.wait_ge(s["val_ready"], g * 4 + (q + 1))
                    tt(hidden[:, i, c], bank[2 + q % 2], hidden[:, i, c], ALU.mult).then_inc(s["gated"], 1)
                    dve.wait_ge(s["inner_hi_done"], g * 4 + (q + 1))
                    tt(inner_lo[:, i, c], hidden[:, i, c], inner_hi[:, i, c].bitcast(F32),
                       ALU.subtract).then_inc(s["inner_lo_done"], 1)
                if more:
                    split_unit_low(g * 3 + (J_FFN + 2), 1)

            def add_down(g, tiles=range(TT)):
                for m in range(2 * tiles[0], 2 * tiles[-1] + 2):
                    dve.wait_ge(s["down_ready"], g * 16 + (m + 2))
                    r = x1[:, m // 2, (m % 2) * CH:(m % 2 + 1) * CH]
                    tt(r, bank[4 + m % 4], r, ALU.add).then_inc(s["down_added"], 1)

            dve.wait_ge(s["const_set"], 3)
            ffn(0, True, False)
            with dve.Fori(1, NG - 1) as g:
                own.enter(g - 1, 8)
                ffn(g, True, True)
                own.leave(NG - 2)
            ffn(NG - 1, False, True)
            dve.wait_ge(s["fg_loaded"], 16)
            add_down(NG - 1, range(0, 4))
            rsqrt(2, 0)
            for t in range(TT):
                if t == 4:
                    add_down(NG - 1, range(4, TT))
                    rsqrt(2, 1)
                if t >= 4:
                    dve.wait_ge(out_written[t % 4], 16)
                stt(xs[:, t % 4, :], x1[:, t, :], rstd[:, t:t + 1], fg[:], ALU.mult,
                    ALU.mult).then_inc(s["out_ready"], 1)


def _per_channel(a):
    import numpy as np
    a = np.asarray(a)
    lead = a.shape[:-1]
    a = a.reshape(lead + (a.shape[-1] // P, P))
    return np.ascontiguousarray(np.moveaxis(np.moveaxis(a, -1, 0), -1, 1)).reshape(P, -1)


def _unit(w):
    return w.reshape(KT, P, UC).transpose(1, 0, 2).reshape(P, UW)


def kernel(x, norm1_g, w_in, conv_dw_w, conv_dw_b, conv_ln_g, conv_ln_b, conv_pw_w, conv_pw_b, pool_w, pool_scale,
           w_out, norm2_g, ffn_up, ffn_dw_w, ffn_dw_b, ffn_down, final_g):
    import numpy as np
    import concourse.bacc as bacc
    from concourse.bass_utils import run_bass_kernel_spmd

    f = np.float32
    wi, wo, up, dn = (np.asarray(a)[0] for a in (w_in, w_out, ffn_up, ffn_down))
    win = np.repeat(np.array(POOL_WINDOWS, f), DH)
    fix = (win[None, :] / np.minimum(np.arange(1, PAD + 1, dtype=f)[:, None], win[None, :])).astype(f)
    vec = np.concatenate([_per_channel(np.asarray(a)) for a in (
        norm1_g[0], norm2_g[0], conv_dw_w[0], conv_dw_b[0], conv_ln_g[0], conv_ln_b[0], conv_pw_b[0], pool_scale[0],
        (1 / win).astype(f), fix, ffn_dw_w[0], ffn_dw_b[0])], axis=1)
    q0, k0, v0 = 3 * 256, 3 * 256 + 512, 3 * 256 + 1024
    cols = [wi[:, 256:512], wi[:, 0:256], wi[:, 512:768], wi[:, v0:v0 + 256], wi[:, v0 + 256:v0 + 512]]
    for p in range(PAIRS):
        cols.append(np.concatenate([wi[:, q0 + P * p:q0 + P * (p + 1)], wi[:, k0 + P * p:k0 + P * (p + 1)]], axis=1))
    cols += [wo[:, UC * n:UC * (n + 1)] for n in range(4)]
    stacked = [_unit(c) for c in cols]
    gate = [_unit(up[:, D_FF + UC * g:D_FF + UC * (g + 1)]) for g in range(NG)]
    val = [_unit(up[:, UC * g:UC * (g + 1)]) for g in range(NG)]
    down = [dn[2 * P * g:2 * P * (g + 1)].reshape(2, P, D).transpose(1, 0, 2).reshape(P, 2 * D) for g in range(NG)]
    stacked += [gate[0], val[0]]
    for g in range(NG - 1):
        stacked += [gate[g + 1], down[g], val[g + 1]]
    stacked.append(down[NG - 1])
    bd = np.zeros((P, 2, P), f)
    for grp in range(4):
        r = slice(DH * (grp % 2), DH * (grp % 2 + 1))
        bd[r, grp // 2, r] = np.asarray(pool_w)[0, grp]
    host = {
        "x": np.asarray(x), "vec": vec, "units": np.stack(stacked),
        "conv_pw": np.ascontiguousarray(np.asarray(conv_pw_w)[0].reshape(2, P, D_CONV).transpose(1, 0, 2)),
        "pool_bd": bd, "final_g": np.asarray(final_g).reshape(1, D),
    }
    nc = bacc.Bacc("TRN2", target_bir_lowering=False, num_devices=1)
    arrays = {f"in_{n}": np.ascontiguousarray(a) for n, a in host.items()}
    args = [nc.dram_tensor(n, a.shape, mybir.dt.from_np(a.dtype), kind="ExternalInput").ap() for n, a in arrays.items()]
    out = nc.dram_tensor("out", (1, S, D), F32, kind="ExternalOutput").ap()
    build(nc, *args, out)
    return run_bass_kernel_spmd(nc, [arrays], core_ids=[0]).results[0]["out"]
```

```python
from contextlib import ExitStack

import concourse.bass as bass
from concourse import mybir

F32 = mybir.dt.float32
F32R = mybir.dt.float32r
ALU = mybir.AluOpType
ACT = mybir.ActivationFunctionType

P = 128
S = 1024
D = 1024
KT = D // P
TT = S // P
CH = 512
UC = 256
UW = KT * UC
HEADS = 8
PAIRS = HEADS // 2
DH = 64
CONV_K = 31
POOL_WINDOWS = (2, 4, 8, 16)
PAD = max(POOL_WINDOWS)
D_CONV = 256
D_FF = 2816
FT = D_FF // P
NG = FT // 2
EPS = 1e-6
MASK = -float(2 ** 17)
SCALE = DH ** -0.5

VEC = {}
_at = 0
for _name, _n in (("g1", KT), ("g2", KT), ("conv_w", 2 * CONV_K), ("conv_b", 2), ("ln_g", 2), ("ln_b", 2),
                  ("pw_b", 2), ("pool_scale", 2), ("inv_win", 2), ("count_fix", 2 * PAD),
                  ("ffn_w", 3 * FT), ("ffn_b", FT)):
    VEC[_name] = _at
    _at += _n
NVEC = _at

U_GATE, U_A, U_POOL, U_V0, U_V1, U_QK = 0, 1, 2, 3, 4, 5
U_OUT = U_QK + PAIRS
U_FFN_GATE0, U_FFN_VAL0 = U_OUT + 4, U_OUT + 5
U_FFN = U_FFN_VAL0 + 1
NUNITS = U_FFN + 3 * (NG - 1) + 1
J_MIX = U_OUT + 2
NMIXJ = 4
J_OUT2 = J_MIX + NMIXJ
J_FFN_GATE0 = J_OUT2 + 2
J_FFN_VAL0 = J_FFN_GATE0 + 1
J_FFN = J_FFN_VAL0 + 1
J_DOWN_LAST = J_FFN + 3 * (NG - 1)

PJ_QK0 = 3 * 4 + 2 * TT
PJ_POOL_MM = PJ_QK0 - 1
PJ_LOOP = PJ_QK0 + 4
PJ_OUT = PJ_LOOP + 4 * (PAIRS - 1)


def score_units(i):
    n = max(P * (i + 1), 256)
    if n <= CH:
        return [(0, n)]
    first = CH if n - CH >= 256 else n - 256
    return [(0, first), (first, n - first)]


def unit_index(a, i, u):
    return 12 * a + (i if i < 4 else 4 + 2 * (i - 4) + u)


TAKE = [3 * S] + [S * (st % 3) for st in range(2 * TT - 1)]


def take_before(st):
    return max(x for x in range(st - 16, st) if TAKE[x % 16] == TAKE[st])


def slot_groups(i):
    lo = 1 - i % 2
    slots = list(range(lo, lo + i + 1))
    return [slots[:4], slots[4:]] if len(slots) > 4 else [slots]


def build(nc, x, vec, units, conv_pw, pool_bd, final_g, out):
    qk_dram = nc.dram_tensor("qk_scratch", [PAIRS, 2, P, 2, S], F32).ap()
    v_dram = nc.dram_tensor("v_scratch", [TT, P, HEADS, 2 * DH], F32).ap()
    mix_dram = nc.dram_tensor("mix_scratch", [KT, P, S], F32).ap()
    x_tiles = x.rearrange("b (t p) d -> p (b t) d", p=P)
    out_tiles = out.rearrange("b (t p) d -> (b t) p d", p=P)

    with ExitStack() as ctx:
        def sem(name):
            return ctx.enter_context(nc.semaphore(name))

        def sb(where, name, shape, dt=F32):
            return where.enter_context(nc.sbuf_tensor(name, shape, dt))

        psum = ctx.enter_context(nc.psum_tensor("psum", [P, 8, CH], F32))
        bank = [psum[:, b, :] for b in range(8)]

        act_hi = sb(ctx, "act_hi", [P, KT, S], F32R)
        act_lo = sb(ctx, "act_lo", [P, KT, S], F32R)
        stage = sb(ctx, "stage", [P, UW])
        w_hi = [sb(ctx, f"w_hi{s}", [P, KT, UC], F32R) for s in range(2)]
        w_lo = [sb(ctx, f"w_lo{s}", [P, KT, UC], F32R) for s in range(2)]
        ident = sb(ctx, "ident", [P, P])
        vecs = sb(ctx, "vecs", [P, NVEC])
        ss = sb(ctx, "ss", [P, TT])
        var = sb(ctx, "var", [P, TT])
        root = sb(ctx, "root", [P, TT])
        tmp = sb(ctx, "tmp", [P, TT])
        rstd = sb(ctx, "rstd", [P, TT])

        with ExitStack() as mixers:
            nat = sb(mixers, "nat", [P, 2, 2, CH], F32R)
            ident_r = sb(mixers, "ident_r", [P, P], F32R)
            mask = sb(mixers, "mask", [P, 3 * P], F32R)
            with ExitStack() as norm_x:
                xt = sb(norm_x, "xt", [P, TT, D])
                unused = sb(norm_x, "unused", [P, 2, D])
                mask_f = sb(norm_x, "mask_f", [P, 3 * P])
            with ExitStack() as first:
                pool_in = sb(first, "pool_in", [P, 2, PAD + S])
                win_a = sb(first, "win_a", [P, 2, PAD + S])
                win_b = sb(first, "win_b", [P, 2, PAD + S])
                v_nat = sb(first, "v_nat", [P, 2, 4, 2, DH], F32R)
                pb_f = sb(first, "pb_f", [P, 2, P])
                pb_hi = sb(first, "pb_hi", [P, 2, P], F32R)
                pb_lo = sb(first, "pb_lo", [P, 2, P], F32R)
                pw_f = sb(first, "pw_f", [P, 2, D_CONV])
                ones_r = sb(first, "ones_r", [P, P], F32R)
                pw_hi = sb(first, "pw_hi", [P, 2, D_CONV], F32R)
                pw_lo = sb(first, "pw_lo", [P, 2, D_CONV], F32R)
                conv_u = sb(first, "conv_u", [P, 2, CONV_K - 1 + S])
                ln_root = sb(first, "ln_root", [P, S])
                ln_rstd = sb(first, "ln_rstd", [P, S])
                sig_gate = sb(first, "sig_gate", [P, 2, S])
                conv_acc = sb(first, "conv_acc", [P, 2, S])
                mm_hi = sb(first, "mm_hi", [P, 2, S], F32R)
                mm_lo = sb(first, "mm_lo", [P, 2, S], F32R)
            with ExitStack() as attention:
                qs = [sb(attention, f"qs{a}", [P, S], F32R) for a in range(2)]
                ks = [sb(attention, f"ks{a}", [P, 2, S], F32R) for a in range(2)]
                vs = [sb(attention, f"vs{a}", [P, TT, 2 * DH], F32R) for a in range(2)]
                take = sb(attention, "take", [P, 3 * S + P])
                keep = sb(attention, "keep", [P, 2, S])
                at_hi = sb(attention, "at_hi", [P, 2, TT, 2 * P], F32R)
                at_lo = sb(attention, "at_lo", [P, 2, TT, 2 * P], F32R)
                low_half = sb(attention, "low_half", [P, 2 * P])
                mix_pair = sb(attention, "mix_pair", [P, S])
        with ExitStack() as ffn:
            x1 = sb(ffn, "x1", [P, TT, D])
            xs = sb(ffn, "xs", [P, 4, D])
            wd_hi = sb(ffn, "wd_hi", [P, 2, D], F32R)
            wd_lo = sb(ffn, "wd_lo", [P, 2, D], F32R)
            inner_hi = sb(ffn, "inner_hi", [P, 2, S], F32R)
            inner_lo = sb(ffn, "inner_lo", [P, 2, S], F32R)
            gate_rows = sb(ffn, "gate_rows", [P, 2, 2 + S])
            hidden = sb(ffn, "hidden", [P, 2, S])
            fg = sb(ffn, "fg", [P, D])

        names = """consts_loaded small_loaded const_set masks_ready squared var_ready root_ready act_step dve_step
            pool_step rows_scaled tr_ready norm_hi norm_lo stage_loaded split_hi split_lo job_ready
            small_hi small_lo padded conv_rows conv_tap pool_mean pool_hi pool_lo pool_mm pool_out
            ln_hi ln_lo ln_sum ln_centred ln_sq_hi ln_sq_lo ln_var ln_var_eps ln_rooted ln_scaled ln_affine
            swish_done swish_hi swish_lo pw_mm pw_out mix_written v_hi nat_hi nat_lo
            scores_ready scores_read stick_done tr_at_ready at_hi_done at_lo_done av_done low_copied
            mix_added mix7_hi mix7_lo x1_added
            gate_ready gate_copied gate_conv gelu_done val_ready gated inner_hi_done inner_lo_done down_ready
            down_added fg_loaded out_ready""".split()
        s = {n: sem(n) for n in names}
        x_loaded = [sem(f"x_loaded{q}") for q in range(4)]
        x_again = [sem(f"x_again{q}") for q in range(4)]
        out_written = [sem(f"out_written{q}") for q in range(4)]
        job_read = [sem(f"job_read{b}") for b in range(4)]
        nat_written = [sem(f"nat_written{b}") for b in range(2)]
        v_written = [sem(f"v_written{b}") for b in range(2)]
        qk_loaded = [[sem(f"qk_loaded{a}{c}") for c in range(2)] for a in range(2)]
        v_loaded = [sem(f"v_loaded{a}") for a in range(2)]

        def vcol(name, n=0, k=1):
            return vecs[:, VEC[name] + n:VEC[name] + n + k]

        def ffn_col(name, g, i, k, per):
            if isinstance(g, int):
                return vcol(name, (2 * g + i) * per + k)
            return vecs[:, bass.ds(g * (2 * per) + (VEC[name] + i * per + k), 1)]

        class Own:

            def __init__(self, eng, name):
                self.eng, self.sem, self.base, self.n = eng, s[name], 0, 0

            def done(self, ins):
                self.mark(ins)
                self.wait()

            def mark(self, ins):
                ins.then_inc(self.sem, 1)
                self.n += 1
                return self.n

            def wait(self, back=0):
                self.eng.wait_ge(self.sem, self.base + self.n - back)

            def enter(self, turn, per):
                self.outer, self.per = self.base + self.n, per
                self.base, self.n = turn * per + self.outer, 0

            def leave(self, turns):
                assert self.n == self.per, (self.n, self.per)
                self.base, self.n = self.outer + turns * self.per, 0

        block = ctx.enter_context(nc.Block())

        @block.sync
        def _(sp):
            def load_unit(j, unit):
                sp.wait_ge(s["split_lo"], j)
                sp.dma_start(stage[:], units[unit]).then_inc(s["stage_loaded"], 16)

            for q in range(2):
                sp.dma_start(xt[:, 2 * q:2 * q + 2, :], x_tiles[:, 2 * q:2 * q + 2, :]).then_inc(x_loaded[q], 16)
            sp.dma_start(stage[:], units[0]).then_inc(s["stage_loaded"], 16)
            for q in range(2, 4):
                sp.dma_start(xt[:, 2 * q:2 * q + 2, :], x_tiles[:, 2 * q:2 * q + 2, :]).then_inc(x_loaded[q], 16)
            load_unit(1, 1)
            sp.wait_ge(s["norm_lo"], 2 * KT)
            sp.dma_start(pw_f[:], conv_pw).then_inc(s["small_loaded"], 16)
            sp.dma_start(pb_f[:], pool_bd).then_inc(s["small_loaded"], 16)
            for j in range(2, U_QK + 2):
                load_unit(j, j)

            def load_heads(pair, a, c):
                for b in range(2):
                    sp.wait_ge(nat_written[b], pair * 32 + 16 * (c + 1))
                rows, t = slice(DH * a, DH * (a + 1)), slice(c * CH, (c + 1) * CH)
                for hl in range(2):
                    part = slice(DH * hl, DH * (hl + 1))
                    sp.dma_start(qs[a][part, t].bitcast(F32), qk_dram[pair, 0, rows, hl, t]).then_inc(qk_loaded[a][c], 16)
                    sp.dma_start(ks[a][part, :, t].bitcast(F32), qk_dram[pair, 1, rows, :, t]).then_inc(qk_loaded[a][c], 16)

            def load_values(pair, a):
                sp.dma_start(vs[a][:, :, :].bitcast(F32),
                             v_dram[:, :, 2 * pair + a, :].rearrange("t p c -> p t c")).then_inc(v_loaded[a], 16)

            sp.wait_ge(s["mix_written"], 16 * 2)
            for b in range(2):
                sp.wait_ge(v_written[b], 16 * TT)
            for a in range(2):
                for c in range(2):
                    load_heads(0, a, c)
                load_values(0, a)
            load_unit(U_QK + 2, U_QK + 2)
            with sp.Fori(0, PAIRS - 1) as p:
                sp.wait_ge(s["scores_ready"], p * 24 + 12)
                load_heads(p + 1, 0, 0)
                sp.wait_ge(s["av_done"], p * 8 + 4 + 2)
                load_values(p + 1, 0)
                load_heads(p + 1, 0, 1)
                sp.wait_ge(s["split_lo"], p + (U_QK + 3))
                sp.dma_start(stage[:], units[p + (U_QK + 3)]).then_inc(s["stage_loaded"], 16)
                sp.wait_ge(s["scores_ready"], p * 24 + 24)
                load_heads(p + 1, 1, 0)
                load_heads(p + 1, 1, 1)
                sp.wait_ge(s["av_done"], p * 8 + 8 + 2)
                load_values(p + 1, 1)
            for m in range(NMIXJ):
                n = 2 if m < NMIXJ - 1 else 1
                sp.wait_ge(s["mix_written"], 16 * (4 if m < 2 else 2 * m + n))
                sp.wait_ge(s["split_lo"], J_MIX + m)
                sp.dma_start(stage[:, 0:n * S].rearrange("p (n t) -> p n t", n=n),
                             mix_dram[2 * m:2 * m + n].rearrange("n p t -> p n t")).then_inc(s["stage_loaded"], 16)
            load_unit(J_OUT2, U_OUT + 2)
            sp.wait_ge(s["mix_added"], 8 * PAIRS + 1)
            sp.wait_ge(s["mix7_lo"], 1)
            for q in range(4):
                sp.dma_start(x1[:, 2 * q:2 * q + 2, :], x_tiles[:, 2 * q:2 * q + 2, :]).then_inc(x_again[q], 16)
            sp.dma_start(fg[:], final_g.to_broadcast((P, D))).then_inc(s["fg_loaded"], 16)
            load_unit(J_OUT2 + 1, U_OUT + 3)
            load_unit(J_FFN_GATE0, U_FFN_GATE0)
            load_unit(J_FFN_VAL0, U_FFN_VAL0)
            with sp.Fori(0, NG - 1) as g:
                for r in range(3):
                    sp.wait_ge(s["split_lo"], g * 3 + (J_FFN + r))
                    sp.dma_start(stage[:], units[g * 3 + (U_FFN + r)]).then_inc(s["stage_loaded"], 16)
            load_unit(J_DOWN_LAST, NUNITS - 1)
            for t in range(TT):
                sp.wait_ge(s["out_ready"], t + 1)
                sp.dma_start(out_tiles[t], xs[:, t % 4, :]).then_inc(out_written[t % 4], 16)
            for q in range(4):
                sp.wait_ge(out_written[q], 16 * (TT // 4))

        @block.gpsimd
        def _(pool):
            own = Own(pool, "pool_step")
            own.mark(nc.gpsimd.memset(ident[:], 0.0))
            own.mark(nc.gpsimd.memset(mask_f[:], 0.0))
            own.wait()
            own.done(nc.gpsimd.affine_select(out=ident[:], in_=ident[:], compare_op=ALU.not_equal, fill=1.0, base=0,
                                             pattern=[[-1, P]], channel_multiplier=1))
            own.done(nc.gpsimd.affine_select(out=mask_f[:, P:2 * P], in_=mask_f[:, P:2 * P], compare_op=ALU.is_gt,
                                             fill=MASK, base=0, pattern=[[-1, P]], channel_multiplier=1))
            nc.gpsimd.tensor_copy(ident_r[:], ident[:]).then_inc(s["masks_ready"], 1)
            nc.gpsimd.tensor_copy(mask[:], mask_f[:]).then_inc(s["masks_ready"], 1)

            for name, banks in (("scores_read", 3), ("at_lo_done", 2), ("av_done", 2), ("gate_copied", 2), ("gated", 2),
                                ("down_added", 4), ("tr_at_ready", 1), ("mix_added", 1),
                                ("down_ready", 1)):
                pool.sem_inc(s[name], banks)

            pool.wait_ge(s["norm_lo"], 2 * KT)
            pool.wait_ge(s["masks_ready"], 2)
            nc.gpsimd.memset(conv_u[:, :, 0:CONV_K - 1], 0.0).then_inc(s["padded"], 1)
            own.mark(nc.gpsimd.memset(pool_in[:, :, 0:PAD], 0.0))
            own.mark(nc.gpsimd.memset(win_a[:, :, 0:PAD], 0.0))
            own.mark(nc.gpsimd.memset(win_b[:, :, 0:PAD], 0.0))
            nc.gpsimd.memset(ones_r[:].bitcast(F32), 1.0).then_inc(s["padded"], 1)
            own.wait()
            for b in range(4):
                pool.wait_ge(job_read[b], 3)

            def shifted_sum(dst, src, part, i, lag):
                t0 = PAD
                own.done(nc.gpsimd.tensor_tensor(dst[part, i, t0:t0 + S], src[part, i, t0:t0 + S],
                                                 src[part, i, t0 - lag:t0 - lag + S], ALU.add))
            every, upper = slice(0, P), slice(DH, P)
            shifted_sum(win_a, pool_in, every, 0, 1)
            shifted_sum(win_a, pool_in, every, 1, 1)
            shifted_sum(win_b, win_a, upper, 0, 2)
            shifted_sum(win_b, win_a, every, 1, 2)
            shifted_sum(win_a, win_b, every, 1, 4)
            shifted_sum(win_b, win_a, upper, 1, 8)
            for i in range(2):
                own.done(nc.gpsimd.tensor_copy(win_a[upper, i, PAD:], win_b[upper, i, PAD:]))
            for i in range(2):
                own.done(nc.gpsimd.tensor_tensor(win_a[:, i, PAD:2 * PAD], win_a[:, i, PAD:2 * PAD],
                                                 vcol("count_fix", PAD * i, PAD), ALU.mult))
                own.done(nc.gpsimd.tensor_scalar(win_a[:, i, PAD:], win_a[:, i, PAD:], vcol("inv_win", i), None,
                                                 ALU.mult))
                nc.gpsimd.tensor_tensor(win_b[:, i, PAD:], win_a[:, i, PAD:], pool_in[:, i, PAD:],
                                        ALU.subtract).then_inc(s["pool_mean"], 1)
            pool.wait_ge(s["pool_hi"], 2)
            for i in range(2):
                nc.gpsimd.tensor_tensor(mm_lo[:, i, :], win_b[:, i, PAD:], mm_hi[:, i, :].bitcast(F32),
                                        ALU.subtract).then_inc(s["pool_lo"], 1)

            def write_rows(pair, q):
                pool.wait_ge(s["nat_lo"], pair * 4 + (q + 1))
                pool.dma_start(qk_dram[pair, q % 2, :, :, (q // 2) * CH:(q // 2 + 1) * CH],
                               nat[:, q % 2].bitcast(F32)).then_inc(nat_written[q % 2], 16)

            pool.wait_ge(s["pool_out"], 4)
            for i in range(2):
                pool.dma_start(mix_dram[2 + i], pool_in[:, i, PAD:]).then_inc(s["mix_written"], 16)
            for q in range(4):
                write_rows(0, q)
            pool.wait_ge(s["pw_out"], 4)
            for i in range(2):
                pool.dma_start(mix_dram[i], sig_gate[:, i, :]).then_inc(s["mix_written"], 16)
            pool.wait_ge(s["mix_written"], 64)
            for b in range(2):
                pool.wait_ge(v_written[b], 16 * TT)
            nc.gpsimd.memset(at_hi[:, :, 0, 0:P].bitcast(F32), 0.0).then_inc(s["const_set"], 1)
            nc.gpsimd.memset(at_lo[:, :, 0, 0:P].bitcast(F32), 0.0).then_inc(s["const_set"], 1)
            with pool.Fori(0, PAIRS - 1) as p:
                for q in range(4):
                    write_rows(p + 1, q)
                pool.wait_ge(s["mix_added"], p * 8 + 9)
                pool.dma_start(mix_dram[p + 4], mix_pair[:]).then_inc(s["mix_written"], 16)
            pool.wait_ge(s["mix_added"], 8 * PAIRS + 1)
            pool.wait_ge(s["mix7_lo"], 1)
            nc.gpsimd.memset(gate_rows[:, :, 0:2], 0.0).then_inc(s["const_set"], 1)

        @block.tensor
        def _(pe):
            def norm_transposes(r, h):
                src = xt if r == 0 else xs
                pe.wait_ge(s["rows_scaled"], 8 * r + 4 * h + 4)
                for k in range(KT):
                    n = 16 * r + 8 * h + k
                    if n % 16 >= 4:
                        pe.wait_ge(s["norm_lo"], n - 3)
                    for q in range(4):
                        last = nc.tensor.transpose(bank[4 + k % 4][:, q * P:(q + 1) * P],
                                                   src[:, (4 * h if r == 0 else 0) + q, k * P:(k + 1) * P], ident[:])
                    last.then_inc(s["tr_ready"], 1)

            def products(out, w, a, k, first, last):
                for n, (lhs, rhs) in enumerate(((w[0], a[0]), (w[0], a[1]), (w[1], a[0]))):
                    ins = nc.tensor.matmul(out, lhs, rhs, start=(first and n == 0), stop=(last and n == 2))
                return ins

            def weight_pair(slot, k, i):
                return [w[slot][:, k, i * P:(i + 1) * P] for w in (w_hi, w_lo)]

            def act_pair(k, c):
                return [t[:, k, c * CH:(c + 1) * CH] for t in (act_hi, act_lo)]

            def project(out, slot, q):
                for k in range(KT):
                    ins = products(out, weight_pair(slot, k, q % 2), act_pair(k, q // 2), k, k == 0, k == KT - 1)
                return ins

            def token_rows(out, slot, t):
                for k in range(KT):
                    a = [x_[:, k, t * P:(t + 1) * P] for x_ in (act_hi, act_lo)]
                    w = [w_[slot][:, k, :] for w_ in (w_hi, w_lo)]
                    ins = products(out, a, w, k, k == 0, k == KT - 1)
                return ins

            def channel_sums(b0, c, name):
                for n in range(4):
                    src = (mm_hi, mm_lo)[n % 2]
                    ins = nc.tensor.matmul(bank[b0 + c], ones_r[:], src[:, n // 2, c * CH:(c + 1) * CH],
                                           start=(n == 0), stop=(n == 3))
                ins.then_inc(s[name], 1)

            pe.wait_ge(s["masks_ready"], 2)
            norm_transposes(0, 0)
            for j in range(PJ_LOOP):
                unit, q = (j // 4, j % 4) if j < 12 else (U_V0 + (j - 12) // TT, (j - 12) % TT)
                if j >= PJ_QK0:
                    unit, q = U_QK, j - PJ_QK0
                if j == PJ_QK0 + 2:
                    for c in range(2):
                        pe.wait_ge(s["ln_lo"], 2 * c + 2)
                        channel_sums(4, c, "ln_sum")
                if j == PJ_QK0 + 3:
                    for c in range(2):
                        pe.wait_ge(s["ln_sq_lo"], 2 * c + 2)
                        channel_sums(6, c, "ln_var")
                if q == 0:
                    pe.wait_ge(s["split_lo"], unit + 1)
                if j == 0:
                    pe.wait_ge(s["norm_lo"], KT)
                if j == 2:
                    norm_transposes(0, 1)
                    pe.wait_ge(s["norm_lo"], 2 * KT)
                if j >= 4:
                    pe.wait_ge(job_read[j % 4], j // 4)
                if unit in (U_V0, U_V1):
                    ins = token_rows(bank[j % 4][:, 0:UC], unit % 2, q)
                else:
                    ins = project(bank[j % 4], unit % 2, q)
                ins.then_inc(s["job_ready"], 1)
                if j == PJ_POOL_MM:
                    pe.wait_ge(s["pool_lo"], 2)
                    pe.wait_ge(s["padded"], 2)
                    pe.wait_ge(s["small_lo"], 2)
                    for n in range(4):
                        i, c = n % 2, n // 2
                        ins = products(bank[4 + n][:], (pb_hi[:, i, :], pb_lo[:, i, :]),
                                       [m[:, i, c * CH:(c + 1) * CH] for m in (mm_hi, mm_lo)], 0, True, True)
                        ins.then_inc(s["pool_mm"], 1)

            for n in range(4):
                m, c = n % 2, n // 2
                pe.wait_ge(s["swish_lo"], 2 * c + 2)
                for k in range(2):
                    ins = products(bank[4 + n], [w[:, k, m * P:(m + 1) * P] for w in (pw_hi, pw_lo)],
                                   [t[:, k, c * CH:(c + 1) * CH] for t in (mm_hi, mm_lo)], k, k == 0, k == 1)
                ins.then_inc(s["pw_mm"], 1)

            def scores(p, st):
                a, i = st // 8, st % 8
                if i % 4 == 0:
                    pe.wait_ge(qk_loaded[a][i // 4], p * 64 + 64)
                for u, (c0, n) in enumerate(score_units(i)):
                    idx = unit_index(a, i, u)
                    pe.wait_ge(s["scores_read"], p * 24 + (idx + 1))
                    out = bank[idx % 3]
                    for hl in range(2):
                        if hl == 1 and c0 + n == max(P * (i + 1), 256):
                            m0 = P if i == 0 else 0
                            nc.tensor.matmul(out[:, n - 256:n], ident_r[:], mask[:, m0:m0 + 256],
                                             start=False, stop=False)
                        ins = nc.tensor.matmul(out[:, 0:n], qs[a][:, i * P:(i + 1) * P], ks[a][:, hl, c0:c0 + n],
                                               start=(hl == 0), stop=(hl == 1))
                    ins.then_inc(s["scores_ready"], 1)

            def weight_transposes(p, st):
                a, i = st // 8, st % 8
                pe.wait_ge(s["stick_done"], p * 16 + (st + 1))
                for u, slots in enumerate(slot_groups(i)):
                    idx = unit_index(a, i, u)
                    pe.wait_ge(s["at_lo_done"], p * 24 + (idx + 1))
                    for n, slot in enumerate(slots):
                        b = 2 * (i // 2) + 1 - slot
                        ins = nc.tensor.transpose(bank[3 + idx % 2][:, n * P:(n + 1) * P],
                                                  take[:, TAKE[st] + b * P:TAKE[st] + (b + 1) * P], ident[:])
                    ins.then_inc(s["tr_at_ready"], 1)

            def values(p, c):
                a, j = c // 4, c % 4
                if j == 0:
                    pe.wait_ge(v_loaded[a], p * 16 + 16)
                pe.wait_ge(s["at_lo_done"], p * 24 + (unit_index(a, 2 * j + 1, len(slot_groups(2 * j + 1)) - 1) + 3))
                pe.wait_ge(s["mix_added"], p * 8 + (c + 1))
                for slot in range(2 * j + 2):
                    for t in (at_hi, at_lo):
                        ins = nc.tensor.matmul(bank[5][:, 0:2 * P], vs[a][:, 2 * j + 1 - slot, :], t[:, j % 2, slot, :],
                                               start=(slot == 0 and t is at_hi),
                                               stop=(slot == 2 * j + 1 and t is at_lo))
                ins.then_inc(s["av_done"], 1)

            def next_rows(p, v):
                at = 8 * (v - 2)
                q = at // 24
                if at == 0:
                    pe.wait_ge(s["split_lo"], p + (U_QK + 2))
                if at % 24 == 0:
                    pe.wait_ge(s["nat_lo"], p * 4 + (4 + q - 1))
                for m in range(at % 24, at % 24 + 8):
                    k, n = m // 3, m % 3
                    w, t = weight_pair(0, k, q % 2), act_pair(k, q // 2)
                    ins = nc.tensor.matmul(bank[6 + q % 2], w[n // 2], t[n % 2], start=(m == 0), stop=(m == 23))
                if m == 23:
                    ins.then_inc(s["job_ready"], 1)

            def out_bank(m):
                return bank[6 + m] if m < 2 else bank[(m - 2) % 4]

            def out_products(m, ks):
                for k in ks:
                    t, slot = m % TT, (m // TT) % 2
                    ins = products(out_bank(m)[:, 0:UC], [x_[:, k, t * P:(t + 1) * P] for x_ in (act_hi, act_lo)],
                                   [w_[slot][:, k, :] for w_ in (w_hi, w_lo)], k, k == 0, k == KT - 1)
                return ins

            def early_output(v):
                if v == 10:
                    pe.wait_ge(s["split_lo"], J_MIX + 2)
                if v in (10, 11, 12, 13):
                    out_products((v - 10) // 2, range(2 * (v % 2), 2 * (v % 2) + 2))
                if v == 14:
                    pe.wait_ge(s["split_lo"], J_OUT2)
                    out_products(0, range(4, KT - 1))
                    out_products(1, range(4, KT - 1))
                if v == 15:
                    pe.wait_ge(s["scores_read"], 24 * PAIRS + 3)
                    out_products(2, range(KT - 1))
                if v == 16:
                    out_products(3, range(KT - 1))
                if v == 17:
                    out_products(4, range(KT - 1))

            def step(p, v, last=False):
                if not last or v + 2 < 16:
                    scores(p + (v + 2) // 16, (v + 2) % 16)
                if last:
                    early_output(v)
                if not last and 2 <= v < 14:
                    next_rows(p, v)
                weight_transposes(p + v // 16, v % 16)
                if v % 2 == 0 and v > 0:
                    values(p, v // 2 - 1)

            scores(0, 0)
            scores(0, 1)
            pe.wait_ge(s["pw_out"], 4)
            step(0, 0)
            step(0, 1)
            with pe.Fori(0, PAIRS - 1) as p:
                for v in range(2, 18):
                    step(p, v)
            for v in range(2, 16):
                step(PAIRS - 1, v, last=True)
            early_output(16)
            values(PAIRS - 1, 7)
            early_output(17)

            pe.wait_ge(s["mix7_lo"], 1)
            for m in range(4 * TT):
                if m >= 2 * TT and m % TT == 0:
                    pe.wait_ge(s["split_lo"], J_OUT2 + m // TT - 1)
                if m >= 6:
                    pe.wait_ge(s["x1_added"], m - 3)
                out_products(m, range(KT) if m >= 5 else [KT - 1]).then_inc(s["job_ready"], 1)
                if m == 4 * TT - 3:
                    norm_transposes(1, 0)
            pe.wait_ge(s["x1_added"], 4 * TT)

            def gate(g, job, after_norm=False):
                pe.wait_ge(s["split_lo"], job + 1)
                for q in range(4):
                    if after_norm and q == 2:
                        norm_transposes(1, 1)
                    if after_norm and q % 2 == 0:
                        pe.wait_ge(s["norm_lo"], 16 + 8 * (q // 2) + 8)
                    pe.wait_ge(s["gate_copied"], g * 4 + (q + 1))
                    project(bank[q % 2][:], 0, q).then_inc(s["gate_ready"], 1)

            def val(g):
                pe.wait_ge(s["split_lo"], g * 3 + (J_FFN_VAL0 + 1))
                for q in range(4):
                    pe.wait_ge(s["gated"], g * 4 + (q + 1))
                    project(bank[2 + q % 2][:], 1, q).then_inc(s["val_ready"], 1)

            def down(g, unit_job):
                pe.wait_ge(s["split_lo"], unit_job + 1)
                pe.wait_ge(s["inner_lo_done"], g * 4 + 4)
                for m in range(2 * TT):
                    t, n = m // 2, m % 2
                    pe.wait_ge(s["down_added"], g * 16 + (m + 1))
                    for i in range(2):
                        ins = products(bank[4 + m % 4][:], [x_[:, i, t * P:(t + 1) * P] for x_ in (inner_hi, inner_lo)],
                                       [w[:, i, n * CH:(n + 1) * CH] for w in (wd_hi, wd_lo)], i, i == 0, i == 1)
                    ins.then_inc(s["down_ready"], 1)

            gate(0, J_FFN_GATE0, after_norm=True)
            val(0)
            with pe.Fori(1, NG) as g:
                gate(g, g * 3 + (J_FFN - 3))
                down(g - 1, g * 3 + (J_FFN - 2))
                val(g)
            down(NG - 1, J_DOWN_LAST)

        @block.scalar
        def _(act):
            own = Own(act, "act_step")

            def squares(r, tiles, group, src):
                for t in tiles:
                    if r == 0:
                        act.wait_ge(x_loaded[t // 2], 16)
                        if t >= 2:
                            act.wait_ge(s["squared"], t - 1)
                        over = unused[:, t % 2, :]
                    elif r == 1:
                        act.wait_ge(s["x1_added"], 3 * TT + t + 1)
                        if t >= 4:
                            act.wait_ge(s["tr_ready"], 16 + 8)
                        over = xs[:, t % 4, :]
                    else:
                        act.wait_ge(s["down_added"], 16 * (NG - 1) + 2 * t + 2 + 4)
                        act.wait_ge(s["squared"], 16 + t - 1)
                        over = psum[:, 2 * (t % 2):2 + 2 * (t % 2), :]
                    nc.scalar.activation(over, src[:, t, :], ACT.Square,
                                         accum_out=ss[:, t:t + 1]).then_inc(s["squared"], 1)
                act.wait_ge(s["var_ready"], group + 1)
                cols = slice(tiles[0], tiles[-1] + 1)
                nc.scalar.activation(root[:, cols], var[:, cols], ACT.Sqrt).then_inc(s["root_ready"], 1)

            def norm_high(r, h, gain):
                for k in range(KT):
                    act.wait_ge(s["tr_ready"], 16 * r + 8 * h + k + 1)
                    nc.scalar.activation(act_hi[:, k, h * CH:(h + 1) * CH], bank[4 + k % 4], ACT.Copy,
                                         scale=vcol(gain, k)).then_inc(s["norm_hi"], 1)

            def split_high(job, dst, src=None):
                act.wait_ge(s["stage_loaded"], job * 16 + 16)
                nc.scalar.activation(dst, stage[:] if src is None else src, ACT.Copy).then_inc(s["split_hi"], 1)

            def flat(t):
                return t[:].rearrange("p k n -> p (k n)")

            act.dma_start(vecs[:], vec).then_inc(s["consts_loaded"], 16)
            squares(0, range(0, 4), 0, xt)
            act.wait_ge(s["consts_loaded"], 16)
            norm_high(0, 0, "g1")
            split_high(0, flat(w_hi[0]))
            squares(0, range(4, 8), 1, xt)
            norm_high(0, 1, "g1")
            split_high(1, flat(w_hi[1]))
            act.wait_ge(s["small_loaded"], 32)
            nc.scalar.activation(pw_hi[:], pw_f[:], ACT.Copy).then_inc(s["small_hi"], 1)
            nc.scalar.activation(pb_hi[:], pb_f[:], ACT.Copy).then_inc(s["small_hi"], 1)

            def job(j):
                act.wait_ge(s["job_ready"], j + 1)
                return bank[j % 4]

            for q in range(4):
                nc.scalar.activation(sig_gate[:, q % 2, (q // 2) * CH:(q // 2 + 1) * CH], job(q),
                                     ACT.Sigmoid).then_inc(job_read[q], 1)
            split_high(U_POOL, flat(w_hi[0]))
            act.wait_ge(s["job_ready"], 8)
            split_high(U_V0, flat(w_hi[1]))
            act.wait_ge(s["padded"], 2)
            for q in range(4):
                t0 = PAD + (q // 2) * CH
                nc.scalar.activation(pool_in[:, q % 2, t0:t0 + CH], job(8 + q), ACT.Copy).then_inc(job_read[q], 1)
            split_high(U_V1, flat(w_hi[0]))

            def write_values(n):
                j = 12 + n
                act.wait_ge(job_read[j % 4], j // 4 + 1)
                half, t = n // TT, n % TT
                act.dma_start(v_dram[t, :, 4 * half:4 * half + 4, :],
                              v_nat[:, n % 2].rearrange("p h l c -> p h (l c)").bitcast(F32)
                              ).then_inc(v_written[n % 2], 16)

            for n in range(2 * TT):
                j = 12 + n
                act.wait_ge(s["job_ready"], j + 1)
                if n >= 2:
                    act.wait_ge(v_written[n % 2], 16 * (n // 2))
                nc.scalar.activation(v_nat[:, n % 2, :, 0, :], bank[j % 4][:, 0:UC].rearrange("p (h c) -> p h c", h=4),
                                     ACT.Copy).then_inc(s["v_hi"], 1)
                if n > 0:
                    write_values(n - 1)
                if n == TT - 1:
                    split_high(U_QK, flat(w_hi[1]))
                if n == TT + 3:
                    act.wait_ge(s["pool_mean"], 2)
                    for i in range(2):
                        nc.scalar.activation(mm_hi[:, i, :], win_b[:, i, PAD:], ACT.Copy).then_inc(s["pool_hi"], 1)
                if j == PJ_POOL_MM:
                    for m in range(4):
                        act.wait_ge(s["pool_mm"], m + 1)
                        i, t0 = m % 2, PAD + (m // 2) * CH
                        nc.scalar.activation(pool_in[:, i, t0:t0 + CH], bank[4 + m], ACT.Copy,
                                             scale=vcol("pool_scale", i)).then_inc(s["pool_out"], 1)
            write_values(2 * TT - 1)

            def rows_high(pair, q):
                act.wait_ge(s["job_ready"], pair * 4 + (PJ_QK0 + q + 1))
                act.wait_ge(nat_written[q % 2], pair * 32 + 16 * (q // 2))
                src = bank[q] if isinstance(pair, int) else bank[6 + q % 2]
                nc.scalar.activation(nat[:, q % 2, 0, :], src, ACT.Copy).then_inc(s["nat_hi"], 1)

            parts = [(i, slice(c * CH, (c + 1) * CH)) for c in range(2) for i in range(2)]
            act.wait_ge(s["conv_tap"], 2 * CONV_K)
            for i, t in parts:
                nc.scalar.activation(mm_hi[:, i, t], conv_acc[:, i, t], ACT.Copy).then_inc(s["ln_hi"], 1)
            rows_high(0, 0)
            rows_high(0, 1)
            split_high(U_QK + 1, flat(w_hi[0]))
            for n, (i, t) in enumerate(parts):
                act.wait_ge(s["ln_centred"], n + 1)
                own.done(nc.scalar.activation(sig_gate[:, i, t], conv_acc[:, i, t], ACT.Square))
                nc.scalar.activation(mm_hi[:, i, t], sig_gate[:, i, t], ACT.Copy).then_inc(s["ln_sq_hi"], 1)
            rows_high(0, 2)
            for c in range(2):
                act.wait_ge(s["ln_var_eps"], c + 1)
                nc.scalar.activation(ln_root[:, c * CH:(c + 1) * CH], ln_rstd[:, c * CH:(c + 1) * CH],
                                     ACT.Sqrt).then_inc(s["ln_rooted"], 1)
            for n, (i, t) in enumerate(parts):
                act.wait_ge(s["ln_scaled"], n + 1)
                nc.scalar.activation(sig_gate[:, i, t], conv_acc[:, i, t], ACT.Identity, scale=vcol("ln_g", i),
                                     bias=vcol("ln_b", i)).then_inc(s["ln_affine"], 1)
                nc.scalar.activation(conv_u[:, i, t], conv_acc[:, i, t], ACT.Sigmoid, scale=vcol("ln_g", i),
                                     bias=vcol("ln_b", i)).then_inc(s["ln_affine"], 1)
            rows_high(0, 3)
            for n, (i, t) in enumerate(parts):
                act.wait_ge(s["swish_done"], n + 1)
                nc.scalar.activation(mm_hi[:, i, t], conv_acc[:, i, t], ACT.Copy).then_inc(s["swish_hi"], 1)
            for n in range(4):
                act.wait_ge(s["pw_mm"], n + 1)
                nc.scalar.activation(sig_gate[:, n % 2, (n // 2) * CH:(n // 2 + 1) * CH], bank[4 + n], ACT.Identity,
                                     bias=vcol("pw_b", n % 2)).then_inc(s["pw_out"], 1)

            def squeeze(p, st, first_pair=False):
                a, i = st // 8, st % 8
                prev = take_before(st)
                if not (first_pair and prev < 0):
                    x = prev % 16
                    act.wait_ge(s["tr_at_ready"], p * 24 + (unit_index(x // 8, x % 8, len(slot_groups(x % 8)) - 1) + 2
                                                            - (24 if prev < 0 else 0)))
                if not (first_pair and st < 2):
                    act.wait_ge(s["stick_done"], p * 16 + (st - 1))
                for u, (c0, n) in enumerate(score_units(i)):
                    idx = unit_index(a, i, u)
                    n = min(n, P * (i + 1) - c0)
                    act.wait_ge(s["scores_ready"], p * 24 + (idx + 1))
                    nc.scalar.activation(take[:, TAKE[st] + c0:TAKE[st] + c0 + n], bank[idx % 3][:, 0:n], ACT.Sigmoid, scale=SCALE)
                    nc.scalar.activation(keep[:, st % 2, c0:c0 + n], bank[idx % 3][:, 0:n], ACT.Sigmoid,
                                         scale=-SCALE).then_inc(s["scores_read"], 1)

            def weights_high(p, st):
                a, i = st // 8, st % 8
                j = i // 2
                act.wait_ge(s["av_done"], p * 8 + (4 * a + j + 1))
                for u, slots in enumerate(slot_groups(i)):
                    idx = unit_index(a, i, u)
                    act.wait_ge(s["tr_at_ready"], p * 24 + (idx + 2))
                    nc.scalar.activation(at_hi[:, j % 2, slots[0]:slots[-1] + 1, (i % 2) * P:(i % 2 + 1) * P],
                                         bank[3 + idx % 2][:, 0:P * len(slots)].rearrange("p (s t) -> p s t", t=P),
                                         ACT.Copy).then_inc(s["at_hi_done"], 1)

            def copy_low(p, c):
                a = c // 4
                act.wait_ge(s["av_done"], p * 8 + (c + 3))
                act.wait_ge(s["mix_added"], p * 8 + (c + 1))
                nc.scalar.activation(low_half[DH * a:DH * (a + 1), :], bank[5][DH:P, 0:2 * P],
                                     ACT.Copy).then_inc(s["low_copied"], 1)

            def mix_high(m):
                n = 2 if m < NMIXJ - 1 else 1
                split_high(J_MIX + m, act_hi[:, 2 * m:2 * m + n, :],
                           stage[:, 0:n * S].rearrange("p (n t) -> p n t", n=n))

            def step(p, v, last=False, first_pair=False):
                if not last or v + 2 < 16:
                    squeeze(p + (v + 2) // 16, (v + 2) % 16, first_pair)
                weights_high(p + v // 16, v % 16)
                if v % 2 == 1 and v > 1:
                    copy_low(p, (v - 3) // 2)
                if not last and v in (4, 7, 10, 13):
                    rows_high(p + 1, (4, 7, 10, 13).index(v))
                if not last and v == 15:
                    split_high(p + (U_QK + 2), flat(w_hi[0]))
                if last and v == 2:
                    split_high(U_OUT + 1, flat(w_hi[1]))
                if last and v in (4, 6, 9, 11):
                    mix_high((4, 6, 9, 11).index(v))

            squeeze(0, 0, first_pair=True)
            squeeze(0, 1, first_pair=True)
            act.wait_ge(s["const_set"], 2)
            step(0, 0, first_pair=True)
            step(0, 1, first_pair=True)
            with act.Fori(0, PAIRS - 1) as p:
                for v in range(2, 18):
                    step(p, v)
            for v in range(2, 16):
                step(PAIRS - 1, v, last=True)
            copy_low(PAIRS - 1, 7)
            act.wait_ge(s["mix_added"], 8 * PAIRS + 1)
            nc.scalar.activation(act_hi[:, KT - 1, :], mix_pair[:], ACT.Copy).then_inc(s["mix7_hi"], 1)

            act.wait_ge(s["job_ready"], PJ_OUT + TT)
            split_high(J_OUT2, flat(w_hi[0]))
            act.wait_ge(s["job_ready"], PJ_OUT + 2 * TT)
            split_high(J_OUT2 + 1, flat(w_hi[1]))
            act.wait_ge(s["job_ready"], PJ_OUT + 3 * TT)
            split_high(J_FFN_GATE0, flat(w_hi[0]))
            squares(1, range(0, 4), 2, x1)
            norm_high(1, 0, "g2")
            squares(1, range(4, 8), 3, x1)
            norm_high(1, 1, "g2")
            split_high(J_FFN_VAL0, flat(w_hi[1]))

            def ffn(g, more):
                for q in range(4):
                    act.wait_ge(s["gate_ready"], g * 4 + (q + 1))
                    t0 = 2 + (q // 2) * CH
                    nc.scalar.activation(gate_rows[:, q % 2, t0:t0 + CH], bank[q % 2],
                                         ACT.Copy).then_inc(s["gate_copied"], 1)
                if more:
                    split_high(g * 3 + J_FFN, flat(w_hi[0]))
                for q in range(4):
                    act.wait_ge(s["gate_conv"], g * 4 + (q + 1))
                    h = hidden[:, q % 2, (q // 2) * CH:(q // 2 + 1) * CH]
                    nc.scalar.activation(h, h, ACT.Gelu).then_inc(s["gelu_done"], 1)
                act.wait_ge(s["down_ready"], g * 16 + 1)
                split_high(g * 3 + (J_FFN + 1) if more else J_DOWN_LAST, flat(wd_hi))
                for q in range(4):
                    act.wait_ge(s["gated"], g * 4 + (q + 3))
                    c = slice((q // 2) * CH, (q // 2 + 1) * CH)
                    nc.scalar.activation(inner_hi[:, q % 2, c], hidden[:, q % 2, c],
                                         ACT.Copy).then_inc(s["inner_hi_done"], 1)
                if more:
                    split_high(g * 3 + (J_FFN + 2), flat(w_hi[1]))

            with act.Fori(0, NG - 1) as g:
                ffn(g, True)
            ffn(NG - 1, False)
            for u in range(4):
                squares(2, range(2 * u, 2 * u + 2), 4 + u, x1)

        @block.vector
        def _(dve):
            own = Own(dve, "dve_step")
            tsc, stt, tt = nc.vector.tensor_scalar, nc.vector.scalar_tensor_tensor, nc.vector.tensor_tensor

            def mean_squares(squared, tiles):
                cols = slice(tiles[0], tiles[-1] + 1)
                dve.wait_ge(s["squared"], squared)
                tsc(var[:, cols], ss[:, cols], 1.0 / D, EPS, ALU.mult, ALU.add).then_inc(s["var_ready"], 1)

            def inverse_roots(group, tiles):
                cols = slice(tiles[0], tiles[-1] + 1)
                dve.wait_ge(s["root_ready"], group + 1)
                own.done(nc.vector.reciprocal(tmp[:, cols], root[:, cols]))
                own.done(tt(tmp[:, cols], tmp[:, cols], var[:, cols], ALU.mult))
                own.done(tt(tmp[:, cols], tmp[:, cols], root[:, cols], ALU.add))
                own.done(tsc(tmp[:, cols], tmp[:, cols], 0.5, None, ALU.mult))
                own.done(nc.vector.reciprocal(rstd[:, cols], tmp[:, cols]))

            def scale_rows(h, dst, src):
                for q in range(4):
                    t = 4 * h + q
                    tsc(dst(t), src[:, t, :], rstd[:, t:t + 1], None, ALU.mult).then_inc(s["rows_scaled"], 1)

            def norm_low(r, h, gain):
                for k in range(KT):
                    dve.wait_ge(s["norm_hi"], 16 * r + 8 * h + k + 1)
                    c = slice(h * CH, (h + 1) * CH)
                    stt(act_lo[:, k, c], bank[4 + k % 4], vcol(gain, k), act_hi[:, k, c].bitcast(F32),
                        ALU.mult, ALU.subtract).then_inc(s["norm_lo"], 1)

            def flat(t):
                return t[:].rearrange("p k n -> p (k n)")

            def split_low(job, lo, hi, src=None):
                dve.wait_ge(s["split_hi"], job + 1)
                tt(lo, stage[:] if src is None else src, hi.bitcast(F32), ALU.subtract).then_inc(s["split_lo"], 1)

            def split_unit_low(job, slot):
                split_low(job, flat(w_lo[slot]), flat(w_hi[slot]))

            for h in range(2):
                tiles = range(4 * h, 4 * h + 4)
                mean_squares(4 * h + 4, tiles)
                inverse_roots(h, tiles)
                scale_rows(h, lambda t: xt[:, t, :], xt)
                dve.wait_ge(s["consts_loaded"], 16)
                norm_low(0, h, "g1")
                split_unit_low(h, h)
            for n, (f, hi, lo) in enumerate(((pw_f, pw_hi, pw_lo), (pb_f, pb_hi, pb_lo))):
                dve.wait_ge(s["small_hi"], n + 1)
                tt(lo[:], f[:], hi[:].bitcast(F32), ALU.subtract).then_inc(s["small_lo"], 1)
            split_unit_low(U_POOL, 0)

            dve.wait_ge(s["padded"], 1)
            for q in range(4):
                i, c = q % 2, q // 2
                dve.wait_ge(job_read[q], 1)
                dve.wait_ge(s["job_ready"], 4 + q + 1)
                tt(conv_u[:, i, CONV_K - 1 + c * CH:CONV_K - 1 + (c + 1) * CH], bank[q],
                   sig_gate[:, i, c * CH:(c + 1) * CH], ALU.mult).then_inc(job_read[q], 1)
            for q in range(4):
                dve.wait_ge(job_read[q], 2)

            def conv_taps(first, count):
                for n in range(first, first + count):
                    i, k = n % 2, n // 2
                    rows, w = conv_u[:, i, k:k + S], vcol("conv_w", i * CONV_K + k)
                    if k == 0:
                        ins = tsc(conv_acc[:, i, :], rows, w, vcol("conv_b", i), ALU.mult, ALU.add)
                    else:
                        dve.wait_ge(s["conv_tap"], n - 1)
                        ins = stt(conv_acc[:, i, :], rows, w, conv_acc[:, i, :], ALU.mult, ALU.add)
                    ins.then_inc(s["conv_tap"], 1)

            conv_taps(0, 2)
            split_unit_low(U_V0, 1)
            conv_taps(2, 12)
            split_unit_low(U_V1, 0)
            for n in range(2 * TT):
                j = 12 + n
                if n == TT:
                    split_unit_low(U_QK, 1)
                dve.wait_ge(s["v_hi"], n + 1)
                tt(v_nat[:, n % 2, :, 1, :], bank[j % 4][:, 0:UC].rearrange("p (h c) -> p h c", h=4),
                   v_nat[:, n % 2, :, 0, :].bitcast(F32), ALU.subtract).then_inc(job_read[j % 4], 1)
                conv_taps(14 + 3 * n, 3)

            def rows_low(pair, q):
                dve.wait_ge(s["nat_hi"], pair * 4 + (q + 1))
                src = bank[q] if isinstance(pair, int) else bank[6 + q % 2]
                tt(nat[:, q % 2, 1, :], src, nat[:, q % 2, 0, :].bitcast(F32), ALU.subtract).then_inc(s["nat_lo"], 1)

            parts = [(i, slice(c * CH, (c + 1) * CH)) for c in range(2) for i in range(2)]

            def low_of(name_in, name_out, src):
                for n, (i, t) in enumerate(parts):
                    dve.wait_ge(s[name_in], n + 1)
                    tt(mm_lo[:, i, t], src[:, i, t], mm_hi[:, i, t].bitcast(F32), ALU.subtract).then_inc(s[name_out], 1)

            low_of("ln_hi", "ln_lo", conv_acc)
            rows_low(0, 0)
            rows_low(0, 1)
            for n, (i, t) in enumerate(parts):
                dve.wait_ge(s["ln_sum"], n // 2 + 1)
                a = conv_acc[:, i, t]
                stt(a, bank[4 + n // 2], -1.0 / D_CONV, a, ALU.mult, ALU.add).then_inc(s["ln_centred"], 1)
            low_of("ln_sq_hi", "ln_sq_lo", sig_gate)
            split_unit_low(U_QK + 1, 0)
            rows_low(0, 2)
            for c in range(2):
                dve.wait_ge(s["ln_var"], c + 1)
                tsc(ln_rstd[:, c * CH:(c + 1) * CH], bank[6 + c], 1.0 / D_CONV, EPS, ALU.mult,
                    ALU.add).then_inc(s["ln_var_eps"], 1)
            for c in range(2):
                t = slice(c * CH, (c + 1) * CH)
                dve.wait_ge(s["ln_rooted"], c + 1)
                own.done(nc.vector.reciprocal(ln_rstd[:, t], ln_root[:, t]))
                for i in range(2):
                    tt(conv_acc[:, i, t], conv_acc[:, i, t], ln_rstd[:, t], ALU.mult).then_inc(s["ln_scaled"], 1)
            for n, (i, t) in enumerate(parts):
                dve.wait_ge(s["ln_affine"], 2 * n + 2)
                tt(conv_acc[:, i, t], sig_gate[:, i, t], conv_u[:, i, t], ALU.mult).then_inc(s["swish_done"], 1)
            low_of("swish_hi", "swish_lo", conv_acc)
            rows_low(0, 3)

            def stick(p, st):
                a, i = st // 8, st % 8
                n = P * (i + 1)
                dve.wait_ge(s["scores_read"], p * 24 + (unit_index(a, i, len(score_units(i)) - 1) + 4))
                back = keep[:, st % 2, 0:n][:, ::-1]
                own.done(nc.vector.tensor_tensor_scan(back, back, back, 1.0, ALU.mult, ALU.bypass))
                rows = take[:, TAKE[st]:TAKE[st] + n - 1]
                tt(rows, rows, keep[:, st % 2, 1:n],
                   ALU.mult).then_inc(s["stick_done"], 1)

            def weights_low(p, st):
                a, i = st // 8, st % 8
                j = i // 2
                for u, slots in enumerate(slot_groups(i)):
                    idx = unit_index(a, i, u)
                    dve.wait_ge(s["at_hi_done"], p * 24 + (idx + 1))
                    where = (slice(None), j % 2, slice(slots[0], slots[-1] + 1), slice((i % 2) * P, (i % 2 + 1) * P))
                    tt(at_lo[where], bank[3 + idx % 2][:, 0:P * len(slots)].rearrange("p (s t) -> p s t", t=P),
                       at_hi[where].bitcast(F32), ALU.subtract).then_inc(s["at_lo_done"], 1)

            def add_low(p, c):
                a, j = c // 4, c % 4
                dve.wait_ge(s["low_copied"], p * 8 + (c + 1))
                if c == 0:
                    dve.wait_ge(s["mix_written"], p * 16 + 16 * 4)
                rows = slice(DH * a, DH * (a + 1))
                tt(mix_pair[rows, 2 * P * j:2 * P * (j + 1)], bank[5][0:DH, 0:2 * P], low_half[rows, :],
                   ALU.add).then_inc(s["mix_added"], 1)

            def mix_low(m):
                n = 2 if m < NMIXJ - 1 else 1
                split_low(J_MIX + m, act_lo[:, 2 * m:2 * m + n, :], act_hi[:, 2 * m:2 * m + n, :],
                          stage[:, 0:n * S].rearrange("p (n t) -> p n t", n=n))

            def step(p, v, last=False):
                if not last or v + 1 < 16:
                    stick(p + (v + 1) // 16, (v + 1) % 16)
                weights_low(p + v // 16, v % 16)
                if v % 2 == 1 and v > 1:
                    add_low(p, (v - 3) // 2)
                if not last and v in (4, 7, 10, 13):
                    rows_low(p + 1, (4, 7, 10, 13).index(v))
                if not last and v == 15:
                    split_unit_low(p + (U_QK + 2), 0)
                if last and v == 2:
                    split_unit_low(U_OUT + 1, 1)
                if last and v in (4, 6, 9, 11):
                    mix_low((4, 6, 9, 11).index(v))

            stick(0, 0)
            step(0, 0)
            step(0, 1)
            with dve.Fori(0, PAIRS - 1) as p:
                own.enter(p, 16)
                for v in range(2, 18):
                    step(p, v)
                own.leave(PAIRS - 1)
            for v in range(2, 16):
                step(PAIRS - 1, v, last=True)
            add_low(PAIRS - 1, 7)
            dve.wait_ge(s["mix7_hi"], 1)
            tt(act_lo[:, KT - 1, :], mix_pair[:], act_hi[:, KT - 1, :].bitcast(F32), ALU.subtract).then_inc(s["mix7_lo"], 1)

            for m in range(4 * TT):
                n, t = m // TT, m % TT
                if m == TT:
                    split_unit_low(J_OUT2, 0)
                if m == 2 * TT:
                    split_unit_low(J_OUT2 + 1, 1)
                if m == 3 * TT:
                    split_unit_low(J_FFN_GATE0, 0)
                if n == 0 and t % 2 == 0:
                    dve.wait_ge(x_again[t // 2], 16)
                dve.wait_ge(s["job_ready"], PJ_OUT + m + 1)
                r = x1[:, t, n * UC:(n + 1) * UC]
                b = 6 + m if m < 2 else (m - 2) % 4
                tt(r, bank[b][:, 0:UC], r, ALU.add).then_inc(s["x1_added"], 1)
                if m == 3 * TT + 3:
                    mean_squares(8 + 4, range(0, 4))
                    inverse_roots(2, range(0, 4))
                    scale_rows(0, lambda t: xs[:, t % 4, :], x1)
                if m == 4 * TT - 3:
                    norm_low(1, 0, "g2")
            mean_squares(8 + 8, range(4, 8))
            inverse_roots(3, range(4, 8))
            scale_rows(1, lambda t: xs[:, t % 4, :], x1)
            norm_low(1, 1, "g2")
            split_unit_low(J_FFN_VAL0, 1)

            def ffn(g, more, down):
                for q in range(4):
                    i, c0 = q % 2, (q // 2) * CH
                    dve.wait_ge(s["gate_copied"], g * 4 + (q + 3))
                    h = hidden[:, i, c0:c0 + CH]
                    own.done(tsc(h, gate_rows[:, i, c0:c0 + CH], ffn_col("ffn_w", g, i, 0, 3),
                                 ffn_col("ffn_b", g, i, 0, 1), ALU.mult, ALU.add))
                    own.done(stt(h, gate_rows[:, i, c0 + 1:c0 + 1 + CH], ffn_col("ffn_w", g, i, 1, 3), h,
                                 ALU.mult, ALU.add))
                    stt(h, gate_rows[:, i, c0 + 2:c0 + 2 + CH], ffn_col("ffn_w", g, i, 2, 3), h,
                        ALU.mult, ALU.add).then_inc(s["gate_conv"], 1)
                if more:
                    split_unit_low(g * 3 + J_FFN, 0)
                if down:
                    add_down(g - 1)
                split_low(g * 3 + (J_FFN + 1) if more else J_DOWN_LAST, flat(wd_lo), flat(wd_hi))
                for q in range(4):
                    i, c = q % 2, slice((q // 2) * CH, (q // 2 + 1) * CH)
                    dve.wait_ge(s["gelu_done"], g * 4 + (q + 1))
                    dve.wait_ge(s["val_ready"], g * 4 + (q + 1))
                    tt(hidden[:, i, c], bank[2 + q % 2], hidden[:, i, c], ALU.mult).then_inc(s["gated"], 1)
                    dve.wait_ge(s["inner_hi_done"], g * 4 + (q + 1))
                    tt(inner_lo[:, i, c], hidden[:, i, c], inner_hi[:, i, c].bitcast(F32),
                       ALU.subtract).then_inc(s["inner_lo_done"], 1)
                if more:
                    split_unit_low(g * 3 + (J_FFN + 2), 1)

            def add_down(g, tiles=range(TT)):
                for m in range(2 * tiles[0], 2 * tiles[-1] + 2):
                    dve.wait_ge(s["down_ready"], g * 16 + (m + 2))
                    r = x1[:, m // 2, (m % 2) * CH:(m % 2 + 1) * CH]
                    tt(r, bank[4 + m % 4], r, ALU.add).then_inc(s["down_added"], 1)

            dve.wait_ge(s["const_set"], 3)
            ffn(0, True, False)
            with dve.Fori(1, NG - 1) as g:
                own.enter(g - 1, 8)
                ffn(g, True, True)
                own.leave(NG - 2)
            ffn(NG - 1, False, True)
            dve.wait_ge(s["fg_loaded"], 16)

            def mean(u):
                mean_squares(16 + 2 * u + 2, range(2 * u, 2 * u + 2))

            def finish(u):
                inverse_roots(4 + u, range(2 * u, 2 * u + 2))
                for t in range(2 * u, 2 * u + 2):
                    if t >= 4:
                        dve.wait_ge(out_written[t % 4], 16)
                    stt(xs[:, t % 4, :], x1[:, t, :], rstd[:, t:t + 1], fg[:], ALU.mult,
                        ALU.mult).then_inc(s["out_ready"], 1)

            add_down(NG - 1, range(0, 2))
            for u in range(1, 4):
                add_down(NG - 1, range(2 * u, 2 * u + 2))
                if u > 1:
                    finish(u - 2)
                mean(u - 1)
            finish(2)
            mean(3)
            finish(3)


def _per_channel(a):
    import numpy as np
    a = np.asarray(a)
    lead = a.shape[:-1]
    a = a.reshape(lead + (a.shape[-1] // P, P))
    return np.ascontiguousarray(np.moveaxis(np.moveaxis(a, -1, 0), -1, 1)).reshape(P, -1)


def _unit(w):
    return w.reshape(KT, P, UC).transpose(1, 0, 2).reshape(P, UW)


def kernel(x, norm1_g, w_in, conv_dw_w, conv_dw_b, conv_ln_g, conv_ln_b, conv_pw_w, conv_pw_b, pool_w, pool_scale,
           w_out, norm2_g, ffn_up, ffn_dw_w, ffn_dw_b, ffn_down, final_g):
    import numpy as np
    import concourse.bacc as bacc
    from concourse.bass_utils import run_bass_kernel_spmd

    f = np.float32
    wi, wo, up, dn = (np.asarray(a)[0] for a in (w_in, w_out, ffn_up, ffn_down))
    win = np.repeat(np.array(POOL_WINDOWS, f), DH)
    fix = (win[None, :] / np.minimum(np.arange(1, PAD + 1, dtype=f)[:, None], win[None, :])).astype(f)
    vec = np.concatenate([_per_channel(np.asarray(a)) for a in (
        norm1_g[0], norm2_g[0], conv_dw_w[0], conv_dw_b[0], conv_ln_g[0], conv_ln_b[0], conv_pw_b[0], pool_scale[0],
        (1 / win).astype(f), fix, ffn_dw_w[0], ffn_dw_b[0])], axis=1)
    q0, k0, v0 = 3 * 256, 3 * 256 + 512, 3 * 256 + 1024
    cols = [wi[:, 256:512], wi[:, 0:256], wi[:, 512:768], wi[:, v0:v0 + 256], wi[:, v0 + 256:v0 + 512]]
    for p in range(PAIRS):
        cols.append(np.concatenate([wi[:, q0 + P * p:q0 + P * (p + 1)], wi[:, k0 + P * p:k0 + P * (p + 1)]], axis=1))
    cols += [wo[:, UC * n:UC * (n + 1)] for n in range(4)]
    stacked = [_unit(c) for c in cols]
    gate = [_unit(up[:, D_FF + UC * g:D_FF + UC * (g + 1)]) for g in range(NG)]
    val = [_unit(up[:, UC * g:UC * (g + 1)]) for g in range(NG)]
    down = [dn[2 * P * g:2 * P * (g + 1)].reshape(2, P, D).transpose(1, 0, 2).reshape(P, 2 * D) for g in range(NG)]
    stacked += [gate[0], val[0]]
    for g in range(NG - 1):
        stacked += [gate[g + 1], down[g], val[g + 1]]
    stacked.append(down[NG - 1])
    bd = np.zeros((P, 2, P), f)
    for grp in range(4):
        r = slice(DH * (grp % 2), DH * (grp % 2 + 1))
        bd[r, grp // 2, r] = np.asarray(pool_w)[0, grp]
    host = {
        "x": np.asarray(x), "vec": vec, "units": np.stack(stacked),
        "conv_pw": np.ascontiguousarray(np.asarray(conv_pw_w)[0].reshape(2, P, D_CONV).transpose(1, 0, 2)),
        "pool_bd": bd, "final_g": np.asarray(final_g).reshape(1, D),
    }
    nc = bacc.Bacc("TRN2", target_bir_lowering=False, num_devices=1)
    arrays = {f"in_{n}": np.ascontiguousarray(a) for n, a in host.items()}
    args = [nc.dram_tensor(n, a.shape, mybir.dt.from_np(a.dtype), kind="ExternalInput").ap() for n, a in arrays.items()]
    out = nc.dram_tensor("out", (1, S, D), F32, kind="ExternalOutput").ap()
    build(nc, *args, out)
    return run_bass_kernel_spmd(nc, [arrays], core_ids=[0]).results[0]["out"]
```

```python
from contextlib import ExitStack

import concourse.bass as bass
from concourse import mybir

F32 = mybir.dt.float32
F32R = mybir.dt.float32r
ALU = mybir.AluOpType
ACT = mybir.ActivationFunctionType

P = 128
S = 1024
D = 1024
KT = D // P
TT = S // P
CH = 512
UC = 256
UW = KT * UC
HEADS = 8
PAIRS = HEADS // 2
DH = 64
CONV_K = 31
POOL_WINDOWS = (2, 4, 8, 16)
PAD = max(POOL_WINDOWS)
D_CONV = 256
D_FF = 2816
FT = D_FF // P
NG = FT // 2
EPS = 1e-6
MASK = -float(2 ** 17)
SCALE = DH ** -0.5

VEC = {}
_at = 0
for _name, _n in (("g1", KT), ("g2", KT), ("conv_w", 2 * CONV_K), ("conv_b", 2), ("ln_g", 2), ("ln_b", 2),
                  ("pw_b", 2), ("pool_scale", 2), ("inv_win", 2), ("count_fix", 2 * PAD),
                  ("ffn_w", 3 * FT), ("ffn_b", FT)):
    VEC[_name] = _at
    _at += _n
NVEC = _at

U_GATE, U_A, U_POOL, U_QK0, U_V0, U_V1 = 0, 1, 2, 3, 4, 5
U_QK = U_V1
U_OUT = U_QK + PAIRS
U_FFN_GATE0, U_FFN_VAL0 = U_OUT + 4, U_OUT + 5
U_FFN = U_FFN_VAL0 + 1
NUNITS = U_FFN + 3 * (NG - 1) + 1
J_MIX = U_OUT + 1
NMIXJ = 4
J_OUT1 = J_MIX + NMIXJ
J_FFN_GATE0 = J_OUT1 + 3
J_FFN_VAL0 = J_FFN_GATE0 + 1
J_FFN = J_FFN_VAL0 + 1
J_DOWN_LAST = J_FFN + 3 * (NG - 1)

CONV_JOBS = ((0, 0), (1, 0), (0, 1), (1, 1))
PJ_POOL = 2 * len(CONV_JOBS)
PJ_QK0 = PJ_POOL + 4
PJ_V = PJ_QK0 + 4
PJ_LOOP = PJ_V + 2 * TT
PJ_OUT = PJ_LOOP + 4 * (PAIRS - 1)


def score_units(i):
    n = max(P * (i + 1), 256)
    if n <= CH:
        return [(0, n)]
    first = CH if n - CH >= 256 else n - 256
    return [(0, first), (first, n - first)]


def unit_index(a, i, u):
    return 12 * a + (i if i < 4 else 4 + 2 * (i - 4) + u)


TAKE = [3 * S] + [S * (st % 3) for st in range(2 * TT - 1)]


def take_before(st):
    return max(x for x in range(st - 16, st) if TAKE[x % 16] == TAKE[st])


def slot_groups(i):
    lo = 1 - i % 2
    slots = list(range(lo, lo + i + 1))
    return [slots[:4], slots[4:]] if len(slots) > 4 else [slots]


def build(nc, x, vec, units, conv_pw, pool_bd, final_g, out):
    qk_dram = nc.dram_tensor("qk_scratch", [PAIRS, 2, P, 2, S], F32).ap()
    v_dram = nc.dram_tensor("v_scratch", [TT, P, HEADS, 2 * DH], F32).ap()
    mix_dram = nc.dram_tensor("mix_scratch", [KT, P, S], F32).ap()
    x_tiles = x.rearrange("b (t p) d -> p (b t) d", p=P)
    out_tiles = out.rearrange("b (t p) d -> (b t) p d", p=P)

    with ExitStack() as ctx:
        def sem(name):
            return ctx.enter_context(nc.semaphore(name))

        def sb(where, name, shape, dt=F32):
            return where.enter_context(nc.sbuf_tensor(name, shape, dt))

        psum = ctx.enter_context(nc.psum_tensor("psum", [P, 8, CH], F32))
        bank = [psum[:, b, :] for b in range(8)]

        act_hi = sb(ctx, "act_hi", [P, KT, S], F32R)
        act_lo = sb(ctx, "act_lo", [P, KT, S], F32R)
        stage = sb(ctx, "stage", [P, UW])
        w_hi = [sb(ctx, f"w_hi{s}", [P, KT, UC], F32R) for s in range(2)]
        w_lo = [sb(ctx, f"w_lo{s}", [P, KT, UC], F32R) for s in range(2)]
        ident = sb(ctx, "ident", [P, P])
        eps = sb(ctx, "eps", [P, 1])
        vecs = sb(ctx, "vecs", [P, NVEC])
        ss = sb(ctx, "ss", [P, TT])
        var = sb(ctx, "var", [P, TT])
        root = sb(ctx, "root", [P, TT])
        tmp = sb(ctx, "tmp", [P, TT])
        rstd = sb(ctx, "rstd", [P, TT])

        with ExitStack() as mixers:
            nat = sb(mixers, "nat", [P, 2, 2, CH], F32R)
            ident_r = sb(mixers, "ident_r", [P, P], F32R)
            mask = sb(mixers, "mask", [P, 3 * P], F32R)
            with ExitStack() as norm_x:
                xt = sb(norm_x, "xt", [P, TT, D])
                unused = sb(norm_x, "unused", [P, 2, D])
                mask_f = sb(norm_x, "mask_f", [P, 3 * P])
            with ExitStack() as first:
                pool_in = sb(first, "pool_in", [P, 2, PAD + S])
                win_a = sb(first, "win_a", [P, 2, PAD + S])
                win_b = sb(first, "win_b", [P, 2, PAD + S])
                v_nat = sb(first, "v_nat", [P, 2, 4, 2, DH], F32R)
                pb_f = sb(first, "pb_f", [P, 2, P])
                pb_hi = sb(first, "pb_hi", [P, 2, P], F32R)
                pb_lo = sb(first, "pb_lo", [P, 2, P], F32R)
                pw_f = sb(first, "pw_f", [P, 2, D_CONV])
                ones_r = sb(first, "ones_r", [P, P], F32R)
                pw_hi = sb(first, "pw_hi", [P, 2, D_CONV], F32R)
                pw_lo = sb(first, "pw_lo", [P, 2, D_CONV], F32R)
                conv_u = sb(first, "conv_u", [P, 2, CONV_K - 1 + S])
                ln_root = sb(first, "ln_root", [P, S])
                ln_rstd = sb(first, "ln_rstd", [P, S])
                conv_acc = sb(first, "conv_acc", [P, 2, S])
                mm_hi = sb(first, "mm_hi", [P, 2, S], F32R)
                mm_lo = sb(first, "mm_lo", [P, 2, S], F32R)
                sig_gate = sb(first, "sig_gate", [P, 2, S])
            with ExitStack() as attention:
                qs = [sb(attention, f"qs{a}", [P, S], F32R) for a in range(2)]
                ks = [sb(attention, f"ks{a}", [P, 2, S], F32R) for a in range(2)]
                vs = [sb(attention, f"vs{a}", [P, TT, 2 * DH], F32R) for a in range(2)]
                take = sb(attention, "take", [P, 3 * S + P])
                keep = sb(attention, "keep", [P, 2, S])
                low_half = sb(attention, "low_half", [P, 2 * P])
                at_hi = sb(attention, "at_hi", [P, 2, TT, 2 * P], F32R)
                at_lo = sb(attention, "at_lo", [P, 2, TT, 2 * P], F32R)
                mix_pair = sb(attention, "mix_pair", [P, S])
        with ExitStack() as ffn:
            x1 = sb(ffn, "x1", [P, TT, D])
            xs = sb(ffn, "xs", [P, 4, D])
            wd_hi = sb(ffn, "wd_hi", [P, 2, D], F32R)
            wd_lo = sb(ffn, "wd_lo", [P, 2, D], F32R)
            inner_hi = sb(ffn, "inner_hi", [P, 2, S], F32R)
            inner_lo = sb(ffn, "inner_lo", [P, 2, S], F32R)
            gate_rows = sb(ffn, "gate_rows", [P, 2, 2 + S])
            hidden = sb(ffn, "hidden", [P, 2, S])
            fg = sb(ffn, "fg", [P, D])

        names = """consts_loaded small_loaded const_set masks_ready squared var_ready root_ready act_step dve_step
            pool_step rows_scaled tr_ready norm_hi norm_lo stage_loaded split_hi split_lo job_ready
            small_hi small_lo padded pool_mean pool_hi pool_lo pool_mm pool_out
            ln_hi ln_lo ln_sum ln_centred ln_sq_hi ln_sq_lo ln_var ln_rooted ln_scaled ln_affine
            swish_done swish_hi swish_lo pw_mm pw_out pool_written mix_written v_hi nat_hi nat_lo
            scores_ready scores_read stick_done tr_at_ready at_hi_done at_lo_done av_done low_copied
            mix_added mix7_hi mix7_lo x1_added
            gate_ready gate_copied gate_conv gelu_done val_ready gated inner_hi_done inner_lo_done down_ready
            down_added fg_loaded out_ready""".split()
        s = {n: sem(n) for n in names}
        x_loaded = [sem(f"x_loaded{q}") for q in range(4)]
        x_again = [sem(f"x_again{q}") for q in range(4)]
        out_written = [sem(f"out_written{q}") for q in range(4)]
        job_read = [sem(f"job_read{b}") for b in range(4)]
        conv_tap = [sem(f"conv_tap{i}") for i in range(2)]
        nat_written = [sem(f"nat_written{b}") for b in range(2)]
        v_written = [sem(f"v_written{b}") for b in range(2)]
        qk_loaded = [[sem(f"qk_loaded{a}{c}") for c in range(2)] for a in range(2)]
        v_loaded = [sem(f"v_loaded{a}") for a in range(2)]

        def vcol(name, n=0, k=1):
            return vecs[:, VEC[name] + n:VEC[name] + n + k]

        def pool_parts(m):
            i, second = m % 2, slice(CH, S)
            return (nat[:, i, 0, :], nat[:, i, 1, :]) if m < 2 else (mm_hi[:, i, second], mm_lo[:, i, second])

        def ffn_col(name, g, i, k, per):
            if isinstance(g, int):
                return vcol(name, (2 * g + i) * per + k)
            return vecs[:, bass.ds(g * (2 * per) + (VEC[name] + i * per + k), 1)]

        class Own:

            def __init__(self, eng, name):
                self.eng, self.sem, self.base, self.n = eng, s[name], 0, 0

            def done(self, ins):
                self.mark(ins)
                self.wait()

            def mark(self, ins):
                ins.then_inc(self.sem, 1)
                self.n += 1
                return self.n

            def wait(self, back=0):
                self.eng.wait_ge(self.sem, self.base + self.n - back)

            def enter(self, turn, per):
                self.outer, self.per = self.base + self.n, per
                self.base, self.n = turn * per + self.outer, 0

            def leave(self, turns):
                assert self.n == self.per, (self.n, self.per)
                self.base, self.n = self.outer + turns * self.per, 0

        block = ctx.enter_context(nc.Block())

        @block.sync
        def _(sp):
            def load_unit(j, unit):
                sp.wait_ge(s["split_lo"], j)
                sp.dma_start(stage[:], units[unit]).then_inc(s["stage_loaded"], 16)

            for q in range(2):
                sp.dma_start(xt[:, 2 * q:2 * q + 2, :], x_tiles[:, 2 * q:2 * q + 2, :]).then_inc(x_loaded[q], 16)
            sp.dma_start(stage[:], units[0]).then_inc(s["stage_loaded"], 16)
            for q in range(2, 4):
                sp.dma_start(xt[:, 2 * q:2 * q + 2, :], x_tiles[:, 2 * q:2 * q + 2, :]).then_inc(x_loaded[q], 16)
            load_unit(1, 1)
            sp.wait_ge(s["norm_lo"], 2 * KT)
            sp.dma_start(pw_f[:], conv_pw).then_inc(s["small_loaded"], 16)
            sp.dma_start(pb_f[:], pool_bd).then_inc(s["small_loaded"], 16)
            for j in range(2, U_QK + 2):
                load_unit(j, j)

            def load_heads(pair, a, c):
                for b in range(2):
                    sp.wait_ge(nat_written[b], pair * 32 + 16 * (c + 1))
                rows, t = slice(DH * a, DH * (a + 1)), slice(c * CH, (c + 1) * CH)
                for hl in range(2):
                    part = slice(DH * hl, DH * (hl + 1))
                    sp.dma_start(qs[a][part, t].bitcast(F32), qk_dram[pair, 0, rows, hl, t]).then_inc(qk_loaded[a][c], 16)
                    sp.dma_start(ks[a][part, :, t].bitcast(F32), qk_dram[pair, 1, rows, :, t]).then_inc(qk_loaded[a][c], 16)

            def load_values(pair, a):
                sp.dma_start(vs[a][:, :, :].bitcast(F32),
                             v_dram[:, :, 2 * pair + a, :].rearrange("t p c -> p t c")).then_inc(v_loaded[a], 16)

            sp.wait_ge(s["pool_written"], 16 * 2)
            for a in range(2):
                for c in range(2):
                    load_heads(0, a, c)
            for b in range(2):
                sp.wait_ge(v_written[b], 16 * TT)
            for a in range(2):
                load_values(0, a)
            with sp.Fori(0, PAIRS - 1) as p:
                sp.wait_ge(s["split_lo"], p + (U_QK + 2))
                sp.dma_start(stage[:], units[p + (U_QK + 2)]).then_inc(s["stage_loaded"], 16)
                sp.wait_ge(s["scores_ready"], p * 24 + 12)
                load_heads(p + 1, 0, 0)
                sp.wait_ge(s["av_done"], p * 8 + 4 + 2)
                load_values(p + 1, 0)
                load_heads(p + 1, 0, 1)
                sp.wait_ge(s["scores_ready"], p * 24 + 24)
                load_heads(p + 1, 1, 0)
                load_heads(p + 1, 1, 1)
                sp.wait_ge(s["av_done"], p * 8 + 8 + 2)
                load_values(p + 1, 1)
            for m in range(NMIXJ):
                n = 2 if m < NMIXJ - 1 else 1
                sp.wait_ge(s["mix_written"], 16 * (2 if m < 2 else 2 * m + n - 2))
                sp.wait_ge(s["split_lo"], J_MIX + m)
                sp.dma_start(stage[:, 0:n * S].rearrange("p (n t) -> p n t", n=n),
                             mix_dram[2 * m:2 * m + n].rearrange("n p t -> p n t")).then_inc(s["stage_loaded"], 16)
            load_unit(J_OUT1, U_OUT + 1)
            for b in range(2):
                sp.wait_ge(nat_written[b], PAIRS * 32)
            sp.wait_ge(s["scores_ready"], PAIRS * 24)
            for q in range(4):
                sp.dma_start(x1[:, 2 * q:2 * q + 2, :], x_tiles[:, 2 * q:2 * q + 2, :]).then_inc(x_again[q], 16)
            sp.wait_ge(s["mix7_lo"], 1)
            sp.dma_start(fg[:], final_g.to_broadcast((P, D))).then_inc(s["fg_loaded"], 16)
            load_unit(J_OUT1 + 1, U_OUT + 2)
            load_unit(J_OUT1 + 2, U_OUT + 3)
            load_unit(J_FFN_GATE0, U_FFN_GATE0)
            load_unit(J_FFN_VAL0, U_FFN_VAL0)
            with sp.Fori(0, NG - 1) as g:
                for r in range(3):
                    sp.wait_ge(s["split_lo"], g * 3 + (J_FFN + r))
                    sp.dma_start(stage[:], units[g * 3 + (U_FFN + r)]).then_inc(s["stage_loaded"], 16)
            load_unit(J_DOWN_LAST, NUNITS - 1)
            for t in range(TT):
                sp.wait_ge(s["out_ready"], t + 1)
                sp.dma_start(out_tiles[t], xs[:, t % 4, :]).then_inc(out_written[t % 4], 16)
            for q in range(4):
                sp.wait_ge(out_written[q], 16 * (TT // 4))

        @block.gpsimd
        def _(pool):
            own = Own(pool, "pool_step")
            nc.gpsimd.memset(eps[:], EPS).then_inc(s["masks_ready"], 1)
            own.mark(nc.gpsimd.memset(ident[:], 0.0))
            own.mark(nc.gpsimd.memset(mask_f[:], 0.0))
            own.wait()
            own.done(nc.gpsimd.affine_select(out=ident[:], in_=ident[:], compare_op=ALU.not_equal, fill=1.0, base=0,
                                             pattern=[[-1, P]], channel_multiplier=1))
            own.done(nc.gpsimd.affine_select(out=mask_f[:, P:2 * P], in_=mask_f[:, P:2 * P], compare_op=ALU.is_gt,
                                             fill=MASK, base=0, pattern=[[-1, P]], channel_multiplier=1))
            nc.gpsimd.tensor_copy(ident_r[:], ident[:]).then_inc(s["masks_ready"], 1)
            nc.gpsimd.tensor_copy(mask[:], mask_f[:]).then_inc(s["masks_ready"], 1)

            for name, banks in (("scores_read", 3), ("at_lo_done", 2), ("av_done", 2), ("gate_copied", 2), ("gated", 2),
                                ("down_added", 4), ("tr_at_ready", 1), ("mix_added", 1),
                                ("down_ready", 1)):
                pool.sem_inc(s[name], banks)

            pool.wait_ge(s["masks_ready"], 3)
            pool.wait_ge(s["squared"], TT)
            nc.gpsimd.memset(conv_u[:, :, 0:CONV_K - 1], 0.0).then_inc(s["padded"], 1)
            nc.gpsimd.memset(ones_r[:].bitcast(F32), 1.0).then_inc(s["padded"], 1)
            pool.wait_ge(s["norm_lo"], 2 * KT)
            own.mark(nc.gpsimd.memset(pool_in[:, :, 0:PAD], 0.0))
            own.mark(nc.gpsimd.memset(win_a[:, :, 0:PAD], 0.0))
            own.mark(nc.gpsimd.memset(win_b[:, :, 0:PAD], 0.0))
            own.wait()
            def write_rows(pair, q):
                pool.wait_ge(s["nat_lo"], pair * 4 + (q + 1))
                pool.dma_start(qk_dram[pair, q % 2, :, :, (q // 2) * CH:(q // 2 + 1) * CH],
                               nat[:, q % 2].bitcast(F32)).then_inc(nat_written[q % 2], 16)

            for b in range(4):
                pool.wait_ge(job_read[b], 3)

            def shifted_sum(dst, src, part, i, lag):
                t0 = PAD
                own.done(nc.gpsimd.tensor_tensor(dst[part, i, t0:t0 + S], src[part, i, t0:t0 + S],
                                                 src[part, i, t0 - lag:t0 - lag + S], ALU.add))
            every, upper = slice(0, P), slice(DH, P)
            shifted_sum(win_a, pool_in, every, 0, 1)
            shifted_sum(win_a, pool_in, every, 1, 1)
            shifted_sum(win_b, win_a, upper, 0, 2)
            write_rows(0, 0)
            shifted_sum(win_b, win_a, every, 1, 2)
            shifted_sum(win_a, win_b, every, 1, 4)
            write_rows(0, 1)
            shifted_sum(win_b, win_a, upper, 1, 8)
            for i in range(2):
                own.done(nc.gpsimd.tensor_copy(win_a[upper, i, PAD:], win_b[upper, i, PAD:]))
            for i in range(2):
                own.done(nc.gpsimd.tensor_tensor(win_a[:, i, PAD:2 * PAD], win_a[:, i, PAD:2 * PAD],
                                                 vcol("count_fix", PAD * i, PAD), ALU.mult))
                own.done(nc.gpsimd.tensor_scalar(win_a[:, i, PAD:], win_a[:, i, PAD:], vcol("inv_win", i), None,
                                                 ALU.mult))
                nc.gpsimd.tensor_tensor(win_b[:, i, PAD:], win_a[:, i, PAD:], pool_in[:, i, PAD:],
                                        ALU.subtract).then_inc(s["pool_mean"], 1)
                write_rows(0, 2 + i)
            for m in range(4):
                pool.wait_ge(s["pool_hi"], m + 1)
                i, t0 = m % 2, PAD + (m // 2) * CH
                hi, lo = pool_parts(m)
                nc.gpsimd.tensor_tensor(lo, win_b[:, i, t0:t0 + CH], hi.bitcast(F32),
                                        ALU.subtract).then_inc(s["pool_lo"], 1)

            pool.wait_ge(s["pool_out"], 4)
            for i in range(2):
                pool.dma_start(mix_dram[2 + i], pool_in[:, i, PAD:]).then_inc(s["pool_written"], 16)
            pool.wait_ge(s["pw_out"], 4)
            nc.gpsimd.memset(at_hi[:, :, 0, 0:P].bitcast(F32), 0.0).then_inc(s["const_set"], 1)
            nc.gpsimd.memset(at_lo[:, :, 0, 0:P].bitcast(F32), 0.0).then_inc(s["const_set"], 1)
            for i in range(2):
                pool.dma_start(mix_dram[i], sig_gate[:, i, :]).then_inc(s["mix_written"], 16)
            pool.wait_ge(s["mix_written"], 32)
            for b in range(2):
                pool.wait_ge(v_written[b], 16 * TT)
            with pool.Fori(0, PAIRS - 1) as p:
                for q in range(4):
                    write_rows(p + 1, q)
                pool.wait_ge(s["mix_added"], p * 8 + 9)
                pool.dma_start(mix_dram[p + 4], mix_pair[:]).then_inc(s["mix_written"], 16)
            pool.wait_ge(s["mix_added"], 8 * PAIRS + 1)
            pool.wait_ge(s["mix7_lo"], 1)
            nc.gpsimd.memset(gate_rows[:, :, 0:2], 0.0).then_inc(s["const_set"], 1)

        @block.tensor
        def _(pe):
            def norm_transposes(r, h, ks=range(KT)):
                src = xt if r == 0 else xs
                pe.wait_ge(s["rows_scaled"], 8 * r + 4 * h + 4)
                for k in ks:
                    n = 16 * r + 8 * h + k
                    if n % 16 >= 4:
                        pe.wait_ge(s["norm_lo"], n - 3)
                    for q in range(4):
                        last = nc.tensor.transpose(bank[4 + k % 4][:, q * P:(q + 1) * P],
                                                   src[:, (4 * h if r == 0 else 0) + q, k * P:(k + 1) * P], ident[:])
                    last.then_inc(s["tr_ready"], 1)

            def products(out, w, a, k, first, last):
                for n, (lhs, rhs) in enumerate(((w[0], a[0]), (w[0], a[1]), (w[1], a[0]))):
                    ins = nc.tensor.matmul(out, lhs, rhs, start=(first and n == 0), stop=(last and n == 2))
                return ins

            def weight_pair(slot, k, i):
                return [w[slot][:, k, i * P:(i + 1) * P] for w in (w_hi, w_lo)]

            def act_pair(k, c):
                return [t[:, k, c * CH:(c + 1) * CH] for t in (act_hi, act_lo)]

            def project(out, slot, q):
                for k in range(KT):
                    ins = products(out, weight_pair(slot, k, q % 2), act_pair(k, q // 2), k, k == 0, k == KT - 1)
                return ins

            def token_rows(out, slot, t):
                for k in range(KT):
                    a = [x_[:, k, t * P:(t + 1) * P] for x_ in (act_hi, act_lo)]
                    w = [w_[slot][:, k, :] for w_ in (w_hi, w_lo)]
                    ins = products(out, a, w, k, k == 0, k == KT - 1)
                return ins

            def channel_sums(b, c, name):
                for n in range(4):
                    src = (mm_hi, mm_lo)[n % 2]
                    ins = nc.tensor.matmul(bank[b], ones_r[:], src[:, n // 2, c * CH:(c + 1) * CH],
                                           start=(n == 0), stop=(n == 3))
                ins.then_inc(s[name], 1)

            def pointwise(c):
                pe.wait_ge(s["swish_lo"], 2 * c + 2)
                if c == 1:
                    pe.wait_ge(s["pool_out"], 2)
                for m in range(2):
                    for k in range(2):
                        ins = products(bank[6 + m], [w[:, k, m * P:(m + 1) * P] for w in (pw_hi, pw_lo)],
                                       [t[:, k, c * CH:(c + 1) * CH] for t in (mm_hi, mm_lo)], k, k == 0, k == 1)
                    ins.then_inc(s["pw_mm"], 1)

            pe.wait_ge(s["masks_ready"], 3)
            norm_transposes(0, 0)
            units_first = {0: U_GATE, 1: U_A, PJ_POOL: U_POOL, PJ_QK0: U_QK0, PJ_V: U_V0, PJ_V + TT: U_V1}
            for j in range(PJ_LOOP):
                if j in units_first:
                    pe.wait_ge(s["split_lo"], units_first[j] + 1)
                if j == 0:
                    pe.wait_ge(s["norm_lo"], KT)
                if j == 4:
                    pe.wait_ge(s["norm_lo"], 2 * KT)
                if PJ_V <= j < PJ_V + 4:
                    pe.wait_ge(s["nat_lo"], j - PJ_V + 1)
                elif j >= 4:
                    pe.wait_ge(job_read[j % 4], j // 4 - (j > PJ_V))
                if j < PJ_POOL:
                    kind, i = CONV_JOBS[j % 4]
                    ins = project(bank[j % 4], kind, i + 2 * (j // 4))
                elif j < PJ_V:
                    ins = project(bank[j % 4], (j - PJ_POOL) // 4, j % 4)
                else:
                    ins = token_rows(bank[j % 4][:, 0:UC], (j - PJ_V) // TT, (j - PJ_V) % TT)
                ins.then_inc(s["job_ready"], 1)
                if j in (1, 2):
                    norm_transposes(0, 1, range(4 * (j - 1), 4 * j))
                for c, after in enumerate((PJ_QK0 + 2, PJ_V + 7)):
                    if j == after:
                        pe.wait_ge(s["padded"], 2)
                        pe.wait_ge(s["ln_lo"], 2 * c + 2)
                        if c == 1:
                            pe.wait_ge(s["pool_out"], 3)
                        channel_sums(4, c, "ln_sum")
                for c, after in enumerate((PJ_QK0 + 3, PJ_V + 9)):
                    if j == after:
                        pe.wait_ge(s["ln_sq_lo"], 2 * c + 2)
                        if c == 1:
                            pe.wait_ge(s["pool_out"], 4)
                        channel_sums(5, c, "ln_var")
                if j == PJ_V + 4:
                    pointwise(0)
                if j == PJ_V + 5:
                    pe.wait_ge(s["pool_lo"], 4)
                    pe.wait_ge(s["small_lo"], 2)
                    pe.wait_ge(s["pw_out"], 2)
                    for n in range(4):
                        i = n % 2
                        ins = products(bank[(6, 7, 4, 5)[n]], (pb_hi[:, i, :], pb_lo[:, i, :]), pool_parts(n), 0,
                                       True, True)
                        ins.then_inc(s["pool_mm"], 1)
                if j == PJ_V + 13:
                    pointwise(1)

            def scores(p, st):
                a, i = st // 8, st % 8
                if i % 4 == 0:
                    pe.wait_ge(qk_loaded[a][i // 4], p * 64 + 64)
                for u, (c0, n) in enumerate(score_units(i)):
                    idx = unit_index(a, i, u)
                    pe.wait_ge(s["scores_read"], p * 24 + (idx + 1))
                    out = bank[idx % 3]
                    for hl in range(2):
                        if hl == 1 and c0 + n == max(P * (i + 1), 256):
                            m0 = P if i == 0 else 0
                            nc.tensor.matmul(out[:, n - 256:n], ident_r[:], mask[:, m0:m0 + 256],
                                             start=False, stop=False)
                        ins = nc.tensor.matmul(out[:, 0:n], qs[a][:, i * P:(i + 1) * P], ks[a][:, hl, c0:c0 + n],
                                               start=(hl == 0), stop=(hl == 1))
                    ins.then_inc(s["scores_ready"], 1)

            def weight_transposes(p, st):
                a, i = st // 8, st % 8
                pe.wait_ge(s["stick_done"], p * 16 + (st + 1))
                for u, slots in enumerate(slot_groups(i)):
                    idx = unit_index(a, i, u)
                    pe.wait_ge(s["at_lo_done"], p * 24 + (idx + 1))
                    for n, slot in enumerate(slots):
                        b = 2 * (i // 2) + 1 - slot
                        ins = nc.tensor.transpose(bank[3 + idx % 2][:, n * P:(n + 1) * P],
                                                  take[:, TAKE[st] + b * P:TAKE[st] + (b + 1) * P], ident[:])
                    ins.then_inc(s["tr_at_ready"], 1)

            def values(p, c):
                a, j = c // 4, c % 4
                if j == 0:
                    pe.wait_ge(v_loaded[a], p * 16 + 16)
                pe.wait_ge(s["at_lo_done"], p * 24 + (unit_index(a, 2 * j + 1, len(slot_groups(2 * j + 1)) - 1) + 3))
                pe.wait_ge(s["mix_added"], p * 8 + (c + 1))
                for slot in range(2 * j + 2):
                    for t in (at_hi, at_lo):
                        ins = nc.tensor.matmul(bank[5][:, 0:2 * P], vs[a][:, 2 * j + 1 - slot, :], t[:, j % 2, slot, :],
                                               start=(slot == 0 and t is at_hi),
                                               stop=(slot == 2 * j + 1 and t is at_lo))
                ins.then_inc(s["av_done"], 1)

            def next_rows(p, v):
                at = 8 * (v - 2)
                q = at // 24
                if at == 0:
                    pe.wait_ge(s["split_lo"], p + (U_QK + 2))
                if at % 24 == 0:
                    pe.wait_ge(s["nat_lo"], p * 4 + (4 + q - 1))
                for m in range(at % 24, at % 24 + 8):
                    k, n = m // 3, m % 3
                    w, t = weight_pair(0, k, q % 2), act_pair(k, q // 2)
                    ins = nc.tensor.matmul(bank[6 + q % 2], w[n // 2], t[n % 2], start=(m == 0), stop=(m == 23))
                if m == 23:
                    ins.then_inc(s["job_ready"], 1)

            def out_bank(m):
                return bank[6 + m] if m < 2 else bank[(m - 2) % 4]

            def out_products(m, ks):
                for k in ks:
                    t, slot = m % TT, (m // TT) % 2
                    ins = products(out_bank(m)[:, 0:UC], [x_[:, k, t * P:(t + 1) * P] for x_ in (act_hi, act_lo)],
                                   [w_[slot][:, k, :] for w_ in (w_hi, w_lo)], k, k == 0, k == KT - 1)
                return ins

            def early_output(v):
                if v == 10:
                    pe.wait_ge(s["split_lo"], J_MIX + 2)
                if v in (10, 11, 12, 13):
                    out_products((v - 10) // 2, range(2 * (v % 2), 2 * (v % 2) + 2))
                if v == 14:
                    pe.wait_ge(s["split_lo"], J_OUT1)
                    out_products(0, range(4, KT - 1))
                    out_products(1, range(4, KT - 1))
                if v == 15:
                    pe.wait_ge(s["scores_read"], 24 * PAIRS + 3)
                    out_products(2, range(KT - 1))
                if v == 16:
                    out_products(3, range(KT - 1))
                if v == 17:
                    out_products(4, range(KT - 1))

            def step(p, v, last=False):
                if not last or v + 2 < 16:
                    scores(p + (v + 2) // 16, (v + 2) % 16)
                if last:
                    early_output(v)
                weight_transposes(p + v // 16, v % 16)
                if not last and 2 <= v < 14:
                    next_rows(p, v)
                if v % 2 == 0 and v > 0:
                    values(p, v // 2 - 1)

            for b in range(4):
                pe.wait_ge(job_read[b], PJ_LOOP // 4 - 1)
            scores(0, 0)
            scores(0, 1)
            pe.wait_ge(s["pw_out"], 4)
            step(0, 0)
            step(0, 1)
            with pe.Fori(0, PAIRS - 1) as p:
                for v in range(2, 18):
                    step(p, v)
            for v in range(2, 16):
                step(PAIRS - 1, v, last=True)
            early_output(16)
            values(PAIRS - 1, 7)
            early_output(17)

            pe.wait_ge(s["mix7_lo"], 1)
            for m in range(4 * TT):
                if m >= TT and m % TT == 0:
                    pe.wait_ge(s["split_lo"], J_OUT1 + m // TT)
                if m >= 6:
                    pe.wait_ge(s["x1_added"], m - 3)
                out_products(m, range(KT) if m >= 5 else [KT - 1]).then_inc(s["job_ready"], 1)
                if m == 4 * TT - 3:
                    norm_transposes(1, 0)
            pe.wait_ge(s["x1_added"], 4 * TT)

            def gate(g, job, after_norm=False):
                pe.wait_ge(s["split_lo"], job + 1)
                for q in range(4):
                    if after_norm and q == 2:
                        norm_transposes(1, 1)
                    if after_norm and q % 2 == 0:
                        pe.wait_ge(s["norm_lo"], 16 + 8 * (q // 2) + 8)
                    pe.wait_ge(s["gate_copied"], g * 4 + (q + 1))
                    project(bank[q % 2][:], 0, q).then_inc(s["gate_ready"], 1)

            def val(g):
                pe.wait_ge(s["split_lo"], g * 3 + (J_FFN_VAL0 + 1))
                for q in range(4):
                    pe.wait_ge(s["gated"], g * 4 + (q + 1))
                    project(bank[2 + q % 2][:], 1, q).then_inc(s["val_ready"], 1)

            def down(g, unit_job):
                pe.wait_ge(s["split_lo"], unit_job + 1)
                pe.wait_ge(s["inner_lo_done"], g * 4 + 4)
                for m in range(2 * TT):
                    t, n = m // 2, m % 2
                    pe.wait_ge(s["down_added"], g * 16 + (m + 1))
                    for i in range(2):
                        ins = products(bank[4 + m % 4][:], [x_[:, i, t * P:(t + 1) * P] for x_ in (inner_hi, inner_lo)],
                                       [w[:, i, n * CH:(n + 1) * CH] for w in (wd_hi, wd_lo)], i, i == 0, i == 1)
                    ins.then_inc(s["down_ready"], 1)

            gate(0, J_FFN_GATE0, after_norm=True)
            val(0)
            with pe.Fori(1, NG) as g:
                gate(g, g * 3 + (J_FFN - 3))
                down(g - 1, g * 3 + (J_FFN - 2))
                val(g)
            down(NG - 1, J_DOWN_LAST)

        @block.scalar
        def _(act):
            own = Own(act, "act_step")

            def squares(r, tiles, src):
                for t in tiles:
                    if r == 0:
                        act.wait_ge(x_loaded[t // 2], 16)
                        if t >= 2:
                            act.wait_ge(s["squared"], t - 1)
                        over = unused[:, t % 2, :]
                    elif r == 1:
                        act.wait_ge(s["x1_added"], 3 * TT + t + 1)
                        if t >= 4:
                            act.wait_ge(s["tr_ready"], 16 + 8)
                        over = xs[:, t % 4, :]
                    else:
                        act.wait_ge(s["down_added"], 16 * (NG - 1) + 2 * t + 2 + 4)
                        act.wait_ge(s["squared"], 16 + t - 1)
                        over = psum[:, 2 * (t % 2):2 + 2 * (t % 2), :]
                    nc.scalar.activation(over, src[:, t, :], ACT.Square,
                                         accum_out=ss[:, t:t + 1]).then_inc(s["squared"], 1)

            def roots(tiles, group):
                act.wait_ge(s["var_ready"], group + 1)
                cols = slice(tiles[0], tiles[-1] + 1)
                nc.scalar.activation(root[:, cols], var[:, cols], ACT.Sqrt).then_inc(s["root_ready"], 1)

            def norm_high(r, h, gain, ks=range(KT)):
                for k in ks:
                    act.wait_ge(s["tr_ready"], 16 * r + 8 * h + k + 1)
                    nc.scalar.activation(act_hi[:, k, h * CH:(h + 1) * CH], bank[4 + k % 4], ACT.Copy,
                                         scale=vcol(gain, k)).then_inc(s["norm_hi"], 1)

            def split_high(job, dst, src=None):
                act.wait_ge(s["stage_loaded"], job * 16 + 16)
                nc.scalar.activation(dst, stage[:] if src is None else src, ACT.Copy).then_inc(s["split_hi"], 1)

            def flat(t):
                return t[:].rearrange("p k n -> p (k n)")

            act.dma_start(vecs[:], vec).then_inc(s["consts_loaded"], 16)
            squares(0, range(0, 4), xt)
            roots(range(0, 4), 0)
            act.wait_ge(s["consts_loaded"], 16)
            split_high(U_GATE, flat(w_hi[0]))
            squares(0, range(4, 6), xt)
            norm_high(0, 0, "g1")
            squares(0, range(6, 8), xt)
            split_high(U_A, flat(w_hi[1]))
            roots(range(4, 8), 1)

            def job(j):
                act.wait_ge(s["job_ready"], j + 1)
                return bank[j % 4]

            def gates(c, tiles=range(2)):
                for i in tiles:
                    nc.scalar.activation(sig_gate[:, i, c * CH:(c + 1) * CH], job(4 * c + 2 * i),
                                         ACT.Sigmoid).then_inc(job_read[2 * i], 1)

            gates(0, [0])
            norm_high(0, 1, "g1", range(0, 4))
            gates(0, [1])
            norm_high(0, 1, "g1", range(4, 8))
            act.wait_ge(s["small_loaded"], 32)
            nc.scalar.activation(pw_hi[:], pw_f[:], ACT.Copy).then_inc(s["small_hi"], 1)
            nc.scalar.activation(pb_hi[:], pb_f[:], ACT.Copy).then_inc(s["small_hi"], 1)
            gates(1)
            split_high(U_POOL, flat(w_hi[0]))
            act.wait_ge(s["job_ready"], PJ_POOL)
            split_high(U_QK0, flat(w_hi[1]))
            for q in range(4):
                t0 = PAD + (q // 2) * CH
                nc.scalar.activation(pool_in[:, q % 2, t0:t0 + CH], job(PJ_POOL + q),
                                     ACT.Copy).then_inc(job_read[q], 1)
            split_high(U_V0, flat(w_hi[0]))

            def rows_high(pair, q):
                first = isinstance(pair, int)
                act.wait_ge(s["job_ready"], PJ_QK0 + q + 1 if first else pair * 4 + (PJ_LOOP - 4 + q + 1))
                if not first or q > 1:
                    act.wait_ge(nat_written[q % 2], pair * 32 + 16 * (q // 2))
                src = bank[q] if first else bank[6 + q % 2]
                nc.scalar.activation(nat[:, q % 2, 0, :], src, ACT.Copy).then_inc(s["nat_hi"], 1)

            def tiles(c):
                return [(2 * c + i, i, slice(c * CH, (c + 1) * CH)) for i in range(2)]

            def ln_high(c):
                for n, i, t in tiles(c):
                    act.wait_ge(conv_tap[i], CONV_K * (c + 1))
                    nc.scalar.activation(mm_hi[:, i, t], conv_acc[:, i, t], ACT.Copy).then_inc(s["ln_hi"], 1)

            def ln_squares(c):
                for n, i, t in tiles(c):
                    act.wait_ge(s["ln_centred"], n + 1)
                    own.done(nc.scalar.activation(sig_gate[:, i, t], conv_acc[:, i, t], ACT.Square))
                    nc.scalar.activation(mm_hi[:, i, t], sig_gate[:, i, t], ACT.Copy).then_inc(s["ln_sq_hi"], 1)

            def ln_roots(c):
                act.wait_ge(s["ln_var"], c + 1)
                nc.scalar.activation(ln_root[:, c * CH:(c + 1) * CH], bank[5], ACT.Sqrt, scale=1.0 / D_CONV,
                                     bias=eps[:]).then_inc(s["ln_rooted"], 1)

            def swish_parts(c):
                for n, i, t in tiles(c):
                    act.wait_ge(s["ln_scaled"], n + 1)
                    nc.scalar.activation(conv_u[:, i, t], conv_acc[:, i, t], ACT.Sigmoid, scale=vcol("ln_g", i),
                                         bias=vcol("ln_b", i)).then_inc(s["ln_affine"], 1)
                    nc.scalar.activation(sig_gate[:, i, t], conv_acc[:, i, t], ACT.Identity, scale=vcol("ln_g", i),
                                         bias=vcol("ln_b", i)).then_inc(s["ln_affine"], 1)

            def swish_high(c):
                for n, i, t in tiles(c):
                    act.wait_ge(s["swish_done"], n + 1)
                    nc.scalar.activation(mm_hi[:, i, t], conv_acc[:, i, t], ACT.Copy).then_inc(s["swish_hi"], 1)

            def conv_out(c):
                for n, m, t in tiles(c):
                    act.wait_ge(s["pw_mm"], n + 1)
                    nc.scalar.activation(sig_gate[:, m, t], bank[6 + m], ACT.Identity,
                                         bias=vcol("pw_b", m)).then_inc(s["pw_out"], 1)

            ln_high(0)
            rows_high(0, 0)
            rows_high(0, 1)
            ln_squares(0)
            rows_high(0, 2)
            rows_high(0, 3)
            act.wait_ge(s["masks_ready"], 3)
            ln_roots(0)
            split_high(U_V1, flat(w_hi[1]))
            swish_parts(0)
            swish_high(0)

            def write_values(n):
                j = PJ_V + n
                act.wait_ge(job_read[j % 4], j // 4)
                half, t = n // TT, n % TT
                act.dma_start(v_dram[t, :, 4 * half:4 * half + 4, :],
                              v_nat[:, n % 2].rearrange("p h l c -> p h (l c)").bitcast(F32)
                              ).then_inc(v_written[n % 2], 16)

            for n in range(2 * TT):
                j = PJ_V + n
                act.wait_ge(s["job_ready"], j + 1)
                if n >= 2:
                    act.wait_ge(v_written[n % 2], 16 * (n // 2))
                nc.scalar.activation(v_nat[:, n % 2, :, 0, :], bank[j % 4][:, 0:UC].rearrange("p (h c) -> p h c", h=4),
                                     ACT.Copy).then_inc(s["v_hi"], 1)
                if n > 0:
                    write_values(n - 1)
                if n == 1:
                    act.wait_ge(s["pool_mean"], 2)
                    for b in range(2):
                        act.wait_ge(nat_written[b], 32)
                    for m in range(4):
                        i, t0 = m % 2, PAD + (m // 2) * CH
                        nc.scalar.activation(pool_parts(m)[0], win_b[:, i, t0:t0 + CH],
                                             ACT.Copy).then_inc(s["pool_hi"], 1)
                if n == 4:
                    conv_out(0)
                if n == 6:
                    for m in range(4):
                        act.wait_ge(s["pool_mm"], m + 1)
                        i, t0 = m % 2, PAD + (m // 2) * CH
                        nc.scalar.activation(pool_in[:, i, t0:t0 + CH], bank[(6, 7, 4, 5)[m]], ACT.Copy,
                                             scale=vcol("pool_scale", i)).then_inc(s["pool_out"], 1)
                if n == 6:
                    ln_high(1)
                if n == 7:
                    ln_squares(1)
                if n == 9:
                    ln_roots(1)
                if n == 10:
                    swish_parts(1)
                if n == 11:
                    swish_high(1)
                if n == 13:
                    split_high(U_QK + 1, flat(w_hi[0]))
                    conv_out(1)
            write_values(2 * TT - 1)

            def squeeze(p, st, first_pair=False):
                a, i = st // 8, st % 8
                prev = take_before(st)
                if not (first_pair and prev < 0):
                    x = prev % 16
                    act.wait_ge(s["tr_at_ready"], p * 24 + (unit_index(x // 8, x % 8, len(slot_groups(x % 8)) - 1) + 2
                                                            - (24 if prev < 0 else 0)))
                if not (first_pair and st < 2):
                    act.wait_ge(s["stick_done"], p * 16 + (st - 1))
                for u, (c0, n) in enumerate(score_units(i)):
                    idx = unit_index(a, i, u)
                    n = min(n, P * (i + 1) - c0)
                    act.wait_ge(s["scores_ready"], p * 24 + (idx + 1))
                    nc.scalar.activation(take[:, TAKE[st] + c0:TAKE[st] + c0 + n], bank[idx % 3][:, 0:n], ACT.Sigmoid, scale=SCALE)
                    nc.scalar.activation(keep[:, st % 2, c0:c0 + n], bank[idx % 3][:, 0:n], ACT.Sigmoid,
                                         scale=-SCALE).then_inc(s["scores_read"], 1)

            def weights_high(p, st):
                a, i = st // 8, st % 8
                j = i // 2
                act.wait_ge(s["av_done"], p * 8 + (4 * a + j + 1))
                for u, slots in enumerate(slot_groups(i)):
                    idx = unit_index(a, i, u)
                    act.wait_ge(s["tr_at_ready"], p * 24 + (idx + 2))
                    nc.scalar.activation(at_hi[:, j % 2, slots[0]:slots[-1] + 1, (i % 2) * P:(i % 2 + 1) * P],
                                         bank[3 + idx % 2][:, 0:P * len(slots)].rearrange("p (s t) -> p s t", t=P),
                                         ACT.Copy).then_inc(s["at_hi_done"], 1)

            def copy_low(p, c):
                a = c // 4
                act.wait_ge(s["av_done"], p * 8 + (c + 3))
                act.wait_ge(s["mix_added"], p * 8 + (c + 1))
                nc.scalar.activation(low_half[DH * a:DH * (a + 1), :], bank[5][DH:P, 0:2 * P],
                                     ACT.Copy).then_inc(s["low_copied"], 1)

            def mix_high(m):
                n = 2 if m < NMIXJ - 1 else 1
                split_high(J_MIX + m, act_hi[:, 2 * m:2 * m + n, :],
                           stage[:, 0:n * S].rearrange("p (n t) -> p n t", n=n))

            def step(p, v, last=False, first_pair=False):
                if not last or v + 2 < 16:
                    squeeze(p + (v + 2) // 16, (v + 2) % 16, first_pair)
                weights_high(p + v // 16, v % 16)
                if v % 2 == 1 and v > 1:
                    copy_low(p, (v - 3) // 2)
                if not last and v in (4, 7, 10, 13):
                    rows_high(p + 1, (4, 7, 10, 13).index(v))
                if not last and v == 15:
                    split_high(p + (U_QK + 2), flat(w_hi[0]))
                if last and v in (5, 8, 10, 12):
                    mix_high((5, 8, 10, 12).index(v))

            squeeze(0, 0, first_pair=True)
            squeeze(0, 1, first_pair=True)
            act.wait_ge(s["const_set"], 2)
            step(0, 0, first_pair=True)
            step(0, 1, first_pair=True)
            with act.Fori(0, PAIRS - 1) as p:
                for v in range(2, 18):
                    step(p, v)
            for v in range(2, 16):
                step(PAIRS - 1, v, last=True)
            copy_low(PAIRS - 1, 7)
            act.wait_ge(s["mix_added"], 8 * PAIRS + 1)
            nc.scalar.activation(act_hi[:, KT - 1, :], mix_pair[:], ACT.Copy).then_inc(s["mix7_hi"], 1)
            split_high(J_OUT1, flat(w_hi[1]))

            act.wait_ge(s["job_ready"], PJ_OUT + TT)
            split_high(J_OUT1 + 1, flat(w_hi[0]))
            act.wait_ge(s["job_ready"], PJ_OUT + 2 * TT)
            split_high(J_OUT1 + 2, flat(w_hi[1]))
            act.wait_ge(s["job_ready"], PJ_OUT + 3 * TT)
            split_high(J_FFN_GATE0, flat(w_hi[0]))
            squares(1, range(0, 4), x1)
            roots(range(0, 4), 2)
            norm_high(1, 0, "g2")
            squares(1, range(4, 8), x1)
            roots(range(4, 8), 3)

            def copy_gate(g, q):
                act.wait_ge(s["gate_ready"], g * 4 + (q + 1))
                t0 = 2 + (q // 2) * CH
                nc.scalar.activation(gate_rows[:, q % 2, t0:t0 + CH], bank[q % 2],
                                     ACT.Copy).then_inc(s["gate_copied"], 1)

            def ffn(g, more, first=False):
                for q in range(4):
                    if first and q == 2:
                        norm_high(1, 1, "g2")
                        split_high(J_FFN_VAL0, flat(w_hi[1]))
                    copy_gate(g, q)
                if more:
                    split_high(g * 3 + J_FFN, flat(w_hi[0]))
                for q in range(4):
                    act.wait_ge(s["gate_conv"], g * 4 + (q + 1))
                    h = hidden[:, q % 2, (q // 2) * CH:(q // 2 + 1) * CH]
                    nc.scalar.activation(h, h, ACT.Gelu).then_inc(s["gelu_done"], 1)
                if not first:
                    act.wait_ge(s["down_ready"], g * 16 + 1)
                    split_high(g * 3 + (J_FFN + 1) if more else J_DOWN_LAST, flat(wd_hi))
                for q in range(4):
                    act.wait_ge(s["gated"], g * 4 + (q + 3))
                    c = slice((q // 2) * CH, (q // 2 + 1) * CH)
                    nc.scalar.activation(inner_hi[:, q % 2, c], hidden[:, q % 2, c],
                                         ACT.Copy).then_inc(s["inner_hi_done"], 1)
                    if first and q == 1:
                        split_high(J_FFN + 1, flat(wd_hi))
                if more:
                    split_high(g * 3 + (J_FFN + 2), flat(w_hi[1]))

            ffn(0, True, first=True)
            with act.Fori(1, NG - 1) as g:
                ffn(g, True)
            ffn(NG - 1, False)
            for u in range(4):
                squares(2, range(2 * u, 2 * u + 2), x1)
                roots(range(2 * u, 2 * u + 2), 4 + u)

        @block.vector
        def _(dve):
            own = Own(dve, "dve_step")
            tsc, stt, tt = nc.vector.tensor_scalar, nc.vector.scalar_tensor_tensor, nc.vector.tensor_tensor

            def mean_squares(squared, tiles):
                cols = slice(tiles[0], tiles[-1] + 1)
                dve.wait_ge(s["squared"], squared)
                tsc(var[:, cols], ss[:, cols], 1.0 / D, EPS, ALU.mult, ALU.add).then_inc(s["var_ready"], 1)

            def inverse_roots(group, tiles):
                cols = slice(tiles[0], tiles[-1] + 1)
                dve.wait_ge(s["root_ready"], group + 1)
                own.done(nc.vector.reciprocal(tmp[:, cols], root[:, cols]))
                own.done(tt(tmp[:, cols], tmp[:, cols], var[:, cols], ALU.mult))
                own.done(tt(tmp[:, cols], tmp[:, cols], root[:, cols], ALU.add))
                own.done(tsc(tmp[:, cols], tmp[:, cols], 0.5, None, ALU.mult))
                own.done(nc.vector.reciprocal(rstd[:, cols], tmp[:, cols]))

            def scale_rows(h, dst, src):
                for q in range(4):
                    t = 4 * h + q
                    tsc(dst(t), src[:, t, :], rstd[:, t:t + 1], None, ALU.mult).then_inc(s["rows_scaled"], 1)

            def norm_low(r, h, gain, ks=range(KT)):
                for k in ks:
                    dve.wait_ge(s["norm_hi"], 16 * r + 8 * h + k + 1)
                    c = slice(h * CH, (h + 1) * CH)
                    stt(act_lo[:, k, c], bank[4 + k % 4], vcol(gain, k), act_hi[:, k, c].bitcast(F32),
                        ALU.mult, ALU.subtract).then_inc(s["norm_lo"], 1)

            def flat(t):
                return t[:].rearrange("p k n -> p (k n)")

            def split_low(job, lo, hi, src=None):
                dve.wait_ge(s["split_hi"], job + 1)
                tt(lo, stage[:] if src is None else src, hi.bitcast(F32), ALU.subtract).then_inc(s["split_lo"], 1)

            def split_unit_low(job, slot):
                split_low(job, flat(w_lo[slot]), flat(w_hi[slot]))

            def norm_x(h):
                inverse_roots(h, range(4 * h, 4 * h + 4))
                scale_rows(h, lambda t: xt[:, t, :], xt)

            def gated_linear(c, i):
                dve.wait_ge(job_read[2 * i], c + 1)
                dve.wait_ge(s["job_ready"], 4 * c + 2 * i + 1 + 1)
                tt(conv_u[:, i, CONV_K - 1 + c * CH:CONV_K - 1 + (c + 1) * CH], bank[2 * i + 1],
                   sig_gate[:, i, c * CH:(c + 1) * CH], ALU.mult).then_inc(job_read[2 * i + 1], 1)

            taps_left = [[list(range(CONV_K)) for i in range(2)] for c in range(2)]

            def conv_taps(c, count, tiles=(0, 1)):
                for n in range(count):
                    i = tiles[n % len(tiles)]
                    if not taps_left[c][i]:
                        i = 1 - i
                    if not taps_left[c][i]:
                        return
                    k = taps_left[c][i].pop(0)
                    rows, w = conv_u[:, i, c * CH + k:(c + 1) * CH + k], vcol("conv_w", i * CONV_K + k)
                    acc = conv_acc[:, i, c * CH:(c + 1) * CH]
                    if k == 0:
                        dve.wait_ge(job_read[2 * i + 1], c + 1)
                        ins = tsc(acc, rows, w, vcol("conv_b", i), ALU.mult, ALU.add)
                    else:
                        dve.wait_ge(conv_tap[i], CONV_K * c + k)
                        ins = stt(acc, rows, w, acc, ALU.mult, ALU.add)
                    ins.then_inc(conv_tap[i], 1)

            def rows_low(pair, q):
                dve.wait_ge(s["nat_hi"], pair * 4 + (q + 1))
                src = bank[q] if isinstance(pair, int) else bank[6 + q % 2]
                tt(nat[:, q % 2, 1, :], src, nat[:, q % 2, 0, :].bitcast(F32), ALU.subtract).then_inc(s["nat_lo"], 1)

            def tiles(c):
                return [(2 * c + i, i, slice(c * CH, (c + 1) * CH)) for i in range(2)]

            def low_of(c, name_in, name_out, src):
                for n, i, t in tiles(c):
                    dve.wait_ge(s[name_in], n + 1)
                    tt(mm_lo[:, i, t], src[:, i, t], mm_hi[:, i, t].bitcast(F32), ALU.subtract).then_inc(s[name_out], 1)

            def ln_centre(c):
                dve.wait_ge(s["ln_sum"], c + 1)
                for n, i, t in tiles(c):
                    a = conv_acc[:, i, t]
                    stt(a, bank[4], -1.0 / D_CONV, a, ALU.mult, ALU.add).then_inc(s["ln_centred"], 1)

            def ln_scale(c):
                half = slice(c * CH, (c + 1) * CH)
                dve.wait_ge(s["ln_rooted"], c + 1)
                own.done(nc.vector.reciprocal(ln_rstd[:, half], ln_root[:, half]))
                for n, i, t in tiles(c):
                    tt(conv_acc[:, i, t], conv_acc[:, i, t], ln_rstd[:, t], ALU.mult).then_inc(s["ln_scaled"], 1)

            def swish(c):
                for n, i, t in tiles(c):
                    dve.wait_ge(s["ln_affine"], 2 * n + 2)
                    tt(conv_acc[:, i, t], sig_gate[:, i, t], conv_u[:, i, t], ALU.mult).then_inc(s["swish_done"], 1)

            mean_squares(4, range(0, 4))
            norm_x(0)
            dve.wait_ge(s["consts_loaded"], 16)
            split_unit_low(U_GATE, 0)
            norm_low(0, 0, "g1")
            mean_squares(8, range(4, 8))
            split_unit_low(U_A, 1)
            norm_x(1)
            dve.wait_ge(s["padded"], 1)
            gated_linear(0, 0)
            norm_low(0, 1, "g1", range(0, 4))
            conv_taps(0, 5, (0,))
            norm_low(0, 1, "g1", range(4, 8))
            conv_taps(0, 3, (0,))
            gated_linear(0, 1)
            conv_taps(0, 4)
            for n, (f, hi, lo) in enumerate(((pw_f, pw_hi, pw_lo), (pb_f, pb_hi, pb_lo))):
                dve.wait_ge(s["small_hi"], n + 1)
                tt(lo[:], f[:], hi[:].bitcast(F32), ALU.subtract).then_inc(s["small_lo"], 1)
            conv_taps(0, 12)
            gated_linear(1, 0)
            conv_taps(0, 8)
            split_unit_low(U_POOL, 0)
            gated_linear(1, 1)
            conv_taps(0, 2)
            split_unit_low(U_QK0, 1)
            conv_taps(0, 20)
            for n in range(8):
                conv_taps(0, 1, (1,))
                conv_taps(1, 1, (0,))
            conv_taps(0, 2 * CONV_K)
            split_unit_low(U_V0, 0)
            low_of(0, "ln_hi", "ln_lo", conv_acc)
            rows_low(0, 0)
            conv_taps(1, 4)
            rows_low(0, 1)
            ln_centre(0)
            conv_taps(1, 4)
            low_of(0, "ln_sq_hi", "ln_sq_lo", sig_gate)
            conv_taps(1, 3)
            rows_low(0, 2)
            conv_taps(1, 6)
            rows_low(0, 3)
            ln_scale(0)
            split_unit_low(U_V1, 1)
            swish(0)
            conv_taps(1, 3)
            low_of(0, "swish_hi", "swish_lo", conv_acc)
            for n in range(2 * TT):
                j = PJ_V + n
                dve.wait_ge(s["v_hi"], n + 1)
                tt(v_nat[:, n % 2, :, 1, :], bank[j % 4][:, 0:UC].rearrange("p (h c) -> p h c", h=4),
                   v_nat[:, n % 2, :, 0, :].bitcast(F32), ALU.subtract).then_inc(job_read[j % 4], 1)
                conv_taps(1, 6)
                if n == 6:
                    low_of(1, "ln_hi", "ln_lo", conv_acc)
                if n == 7:
                    ln_centre(1)
                if n == 8:
                    low_of(1, "ln_sq_hi", "ln_sq_lo", sig_gate)
                if n == 9:
                    ln_scale(1)
                if n == 11:
                    swish(1)
                    low_of(1, "swish_hi", "swish_lo", conv_acc)
                if n == 13:
                    split_unit_low(U_QK + 1, 0)

            def stick(p, st):
                a, i = st // 8, st % 8
                n = P * (i + 1)
                dve.wait_ge(s["scores_read"], p * 24 + (unit_index(a, i, len(score_units(i)) - 1) + 4))
                back = keep[:, st % 2, 0:n][:, ::-1]
                own.done(nc.vector.tensor_tensor_scan(back, back, back, 1.0, ALU.mult, ALU.bypass))
                rows = take[:, TAKE[st]:TAKE[st] + n - 1]
                tt(rows, rows, keep[:, st % 2, 1:n],
                   ALU.mult).then_inc(s["stick_done"], 1)

            def weights_low(p, st):
                a, i = st // 8, st % 8
                j = i // 2
                for u, slots in enumerate(slot_groups(i)):
                    idx = unit_index(a, i, u)
                    dve.wait_ge(s["at_hi_done"], p * 24 + (idx + 1))
                    where = (slice(None), j % 2, slice(slots[0], slots[-1] + 1), slice((i % 2) * P, (i % 2 + 1) * P))
                    tt(at_lo[where], bank[3 + idx % 2][:, 0:P * len(slots)].rearrange("p (s t) -> p s t", t=P),
                       at_hi[where].bitcast(F32), ALU.subtract).then_inc(s["at_lo_done"], 1)

            def add_low(p, c):
                a, j = c // 4, c % 4
                dve.wait_ge(s["low_copied"], p * 8 + (c + 1))
                if c == 0:
                    dve.wait_ge(s["mix_written"], p * 16 + 16 * 2)
                rows = slice(DH * a, DH * (a + 1))
                tt(mix_pair[rows, 2 * P * j:2 * P * (j + 1)], bank[5][0:DH, 0:2 * P], low_half[rows, :],
                   ALU.add).then_inc(s["mix_added"], 1)

            def mix_low(m):
                n = 2 if m < NMIXJ - 1 else 1
                split_low(J_MIX + m, act_lo[:, 2 * m:2 * m + n, :], act_hi[:, 2 * m:2 * m + n, :],
                          stage[:, 0:n * S].rearrange("p (n t) -> p n t", n=n))

            def step(p, v, last=False):
                if not last or v + 1 < 16:
                    stick(p + (v + 1) // 16, (v + 1) % 16)
                weights_low(p + v // 16, v % 16)
                if v % 2 == 1 and v > 1:
                    add_low(p, (v - 3) // 2)
                if not last and v in (4, 7, 10, 13):
                    rows_low(p + 1, (4, 7, 10, 13).index(v))
                if not last and v == 15:
                    split_unit_low(p + (U_QK + 2), 0)
                if last and v in (5, 8, 10, 12):
                    mix_low((5, 8, 10, 12).index(v))

            stick(0, 0)
            step(0, 0)
            step(0, 1)
            dve.wait_ge(s["mix_written"], 16 * 2)
            with dve.Fori(0, PAIRS - 1) as p:
                own.enter(p, 16)
                for v in range(2, 18):
                    step(p, v)
                own.leave(PAIRS - 1)
            for v in range(2, 16):
                step(PAIRS - 1, v, last=True)
            add_low(PAIRS - 1, 7)
            dve.wait_ge(s["mix7_hi"], 1)
            tt(act_lo[:, KT - 1, :], mix_pair[:], act_hi[:, KT - 1, :].bitcast(F32), ALU.subtract).then_inc(s["mix7_lo"], 1)

            for m in range(4 * TT):
                n, t = m // TT, m % TT
                if m == 3:
                    split_unit_low(J_OUT1, 1)
                if m == TT:
                    split_unit_low(J_OUT1 + 1, 0)
                if m == 2 * TT:
                    split_unit_low(J_OUT1 + 2, 1)
                if m == 3 * TT:
                    split_unit_low(J_FFN_GATE0, 0)
                if n == 0 and t % 2 == 0:
                    dve.wait_ge(x_again[t // 2], 16)
                dve.wait_ge(s["job_ready"], PJ_OUT + m + 1)
                r = x1[:, t, n * UC:(n + 1) * UC]
                b = 6 + m if m < 2 else (m - 2) % 4
                tt(r, bank[b][:, 0:UC], r, ALU.add).then_inc(s["x1_added"], 1)
                if m == 3 * TT + 3:
                    mean_squares(8 + 4, range(0, 4))
                    inverse_roots(2, range(0, 4))
                    scale_rows(0, lambda t: xs[:, t % 4, :], x1)
                if m == 4 * TT - 3:
                    norm_low(1, 0, "g2")
            mean_squares(8 + 8, range(4, 8))
            inverse_roots(3, range(4, 8))
            scale_rows(1, lambda t: xs[:, t % 4, :], x1)

            def ffn(g, more, down):
                for q in range(4):
                    i, c0 = q % 2, (q // 2) * CH
                    if not down and q == 1:
                        norm_low(1, 1, "g2")
                        split_unit_low(J_FFN_VAL0, 1)
                    dve.wait_ge(s["gate_copied"], g * 4 + (q + 3))
                    h = hidden[:, i, c0:c0 + CH]
                    own.done(tsc(h, gate_rows[:, i, c0:c0 + CH], ffn_col("ffn_w", g, i, 0, 3),
                                 ffn_col("ffn_b", g, i, 0, 1), ALU.mult, ALU.add))
                    own.done(stt(h, gate_rows[:, i, c0 + 1:c0 + 1 + CH], ffn_col("ffn_w", g, i, 1, 3), h,
                                 ALU.mult, ALU.add))
                    stt(h, gate_rows[:, i, c0 + 2:c0 + 2 + CH], ffn_col("ffn_w", g, i, 2, 3), h,
                        ALU.mult, ALU.add).then_inc(s["gate_conv"], 1)
                if more:
                    split_unit_low(g * 3 + J_FFN, 0)
                if down:
                    add_down(g - 1)
                    split_low(g * 3 + (J_FFN + 1) if more else J_DOWN_LAST, flat(wd_lo), flat(wd_hi))
                for q in range(4):
                    i, c = q % 2, slice((q // 2) * CH, (q // 2 + 1) * CH)
                    dve.wait_ge(s["gelu_done"], g * 4 + (q + 1))
                    dve.wait_ge(s["val_ready"], g * 4 + (q + 1))
                    tt(hidden[:, i, c], bank[2 + q % 2], hidden[:, i, c], ALU.mult).then_inc(s["gated"], 1)
                    dve.wait_ge(s["inner_hi_done"], g * 4 + (q + 1))
                    tt(inner_lo[:, i, c], hidden[:, i, c], inner_hi[:, i, c].bitcast(F32),
                       ALU.subtract).then_inc(s["inner_lo_done"], 1)
                    if not down and q == 1:
                        split_low(J_FFN + 1, flat(wd_lo), flat(wd_hi))
                if more:
                    split_unit_low(g * 3 + (J_FFN + 2), 1)

            def add_down(g, tiles=range(TT)):
                for m in range(2 * tiles[0], 2 * tiles[-1] + 2):
                    dve.wait_ge(s["down_ready"], g * 16 + (m + 2))
                    r = x1[:, m // 2, (m % 2) * CH:(m % 2 + 1) * CH]
                    tt(r, bank[4 + m % 4], r, ALU.add).then_inc(s["down_added"], 1)

            dve.wait_ge(s["const_set"], 3)
            ffn(0, True, False)
            with dve.Fori(1, NG - 1) as g:
                own.enter(g - 1, 8)
                ffn(g, True, True)
                own.leave(NG - 2)
            ffn(NG - 1, False, True)
            dve.wait_ge(s["fg_loaded"], 16)

            def mean(u):
                mean_squares(16 + 2 * u + 2, range(2 * u, 2 * u + 2))

            def finish(u):
                inverse_roots(4 + u, range(2 * u, 2 * u + 2))
                for t in range(2 * u, 2 * u + 2):
                    if t >= 4:
                        dve.wait_ge(out_written[t % 4], 16)
                    stt(xs[:, t % 4, :], x1[:, t, :], rstd[:, t:t + 1], fg[:], ALU.mult,
                        ALU.mult).then_inc(s["out_ready"], 1)

            add_down(NG - 1, range(0, 2))
            for u in range(1, 4):
                add_down(NG - 1, range(2 * u, 2 * u + 1))
                mean(u - 1)
                add_down(NG - 1, range(2 * u + 1, 2 * u + 2))
                finish(u - 1)
            mean(3)
            finish(3)


def _per_channel(a):
    import numpy as np
    a = np.asarray(a)
    lead = a.shape[:-1]
    a = a.reshape(lead + (a.shape[-1] // P, P))
    return np.ascontiguousarray(np.moveaxis(np.moveaxis(a, -1, 0), -1, 1)).reshape(P, -1)


def _unit(w):
    return w.reshape(KT, P, UC).transpose(1, 0, 2).reshape(P, UW)


def kernel(x, norm1_g, w_in, conv_dw_w, conv_dw_b, conv_ln_g, conv_ln_b, conv_pw_w, conv_pw_b, pool_w, pool_scale,
           w_out, norm2_g, ffn_up, ffn_dw_w, ffn_dw_b, ffn_down, final_g):
    import numpy as np
    import concourse.bacc as bacc
    from concourse.bass_utils import run_bass_kernel_spmd

    f = np.float32
    wi, wo, up, dn = (np.asarray(a)[0] for a in (w_in, w_out, ffn_up, ffn_down))
    win = np.repeat(np.array(POOL_WINDOWS, f), DH)
    fix = (win[None, :] / np.minimum(np.arange(1, PAD + 1, dtype=f)[:, None], win[None, :])).astype(f)
    vec = np.concatenate([_per_channel(np.asarray(a)) for a in (
        norm1_g[0], norm2_g[0], conv_dw_w[0], conv_dw_b[0], conv_ln_g[0], conv_ln_b[0], conv_pw_b[0], pool_scale[0],
        (1 / win).astype(f), fix, ffn_dw_w[0], ffn_dw_b[0])], axis=1)
    q0, k0, v0 = 3 * 256, 3 * 256 + 512, 3 * 256 + 1024
    cols = [wi[:, 256:512], wi[:, 0:256], wi[:, 512:768], wi[:, v0:v0 + 256], wi[:, v0 + 256:v0 + 512]]
    qk = [np.concatenate([wi[:, q0 + P * p:q0 + P * (p + 1)], wi[:, k0 + P * p:k0 + P * (p + 1)]], axis=1)
          for p in range(PAIRS)]
    cols = cols[:U_QK0] + [qk[0]] + cols[U_QK0:] + qk[1:]
    cols += [wo[:, UC * n:UC * (n + 1)] for n in range(4)]
    stacked = [_unit(c) for c in cols]
    gate = [_unit(up[:, D_FF + UC * g:D_FF + UC * (g + 1)]) for g in range(NG)]
    val = [_unit(up[:, UC * g:UC * (g + 1)]) for g in range(NG)]
    down = [dn[2 * P * g:2 * P * (g + 1)].reshape(2, P, D).transpose(1, 0, 2).reshape(P, 2 * D) for g in range(NG)]
    stacked += [gate[0], val[0]]
    for g in range(NG - 1):
        stacked += [gate[g + 1], down[g], val[g + 1]]
    stacked.append(down[NG - 1])
    bd = np.zeros((P, 2, P), f)
    for grp in range(4):
        r = slice(DH * (grp % 2), DH * (grp % 2 + 1))
        bd[r, grp // 2, r] = np.asarray(pool_w)[0, grp]
    host = {
        "x": np.asarray(x), "vec": vec, "units": np.stack(stacked),
        "conv_pw": np.ascontiguousarray(np.asarray(conv_pw_w)[0].reshape(2, P, D_CONV).transpose(1, 0, 2)),
        "pool_bd": bd, "final_g": np.asarray(final_g).reshape(1, D),
    }
    nc = bacc.Bacc("TRN2", target_bir_lowering=False, num_devices=1)
    arrays = {f"in_{n}": np.ascontiguousarray(a) for n, a in host.items()}
    args = [nc.dram_tensor(n, a.shape, mybir.dt.from_np(a.dtype), kind="ExternalInput").ap() for n, a in arrays.items()]
    out = nc.dram_tensor("out", (1, S, D), F32, kind="ExternalOutput").ap()
    build(nc, *args, out)
    return run_bass_kernel_spmd(nc, [arrays], core_ids=[0]).results[0]["out"]
```
